# Optimizing a Trainium2 kernel written in Bass

```python
import math
import jax
import jax.numpy as jnp
from jax import lax
import numpy as np

D_MODEL = 1024
BATCH = 1
SEQ = 128
DEPTH = 2
DEC_BATCH = 1
DEC_SEQ = 256
PAST_LEN = 128

GRID_W = 64
N_MOD = 6
EPS = 1e-6
POOL_WIDTH = 256
POOL_GROUPS = 4
POOL_GROUP_CH = POOL_WIDTH // POOL_GROUPS
POOL_WINDOWS = (2, 4, 8, 16)
SSD_WIDTH = 256
SSD_HEAD_DIM = 64
SSD_HEADS = SSD_WIDTH // SSD_HEAD_DIM
SSD_GROUPS = 2
SSD_STATE = 128
SSD_CONV = 5
SSD_CHUNK = 128
SSD_CONV_CH = SSD_WIDTH + 2 * SSD_GROUPS * SSD_STATE
ATT_HEADS = 4
ATT_HEAD_DIM = 64
ATT_QK = 2 * ATT_HEAD_DIM
ATT_V = 2 * ATT_HEAD_DIM
ATT_WIDTH = ATT_HEADS * ATT_V
Q_BLOCK = 128
ROPE_THETA = 10000.0
MIX_WIDTH = POOL_WIDTH + SSD_WIDTH + ATT_WIDTH
IN_COLS = POOL_WIDTH + SSD_WIDTH + SSD_CONV_CH + 2 * SSD_HEADS + 2 * ATT_HEADS * ATT_QK + ATT_HEADS * ATT_V
PEER_HEADS = 8
PEER_KEYS = 128
PEER_EXPERTS = PEER_KEYS * PEER_KEYS
PEER_TOPK = 16
PEER_QDIM = 256
PEER_HALF = PEER_QDIM // 2
PEER_BLOCK = 128

kernel_name = "hybrid_pool_ssd_diffattn_peer_dit_step"

def rmsnorm(x, w):
    xf = x.astype(jnp.float32)
    y = xf * lax.rsqrt(jnp.mean(xf * xf, axis=-1, keepdims=True) + EPS)
    return y.astype(x.dtype) * w

def adaln(cond, mod_w, mod_b):
    m = jax.nn.silu(cond) @ mod_w + mod_b
    if m.ndim == 2:
        m = m[:, None, :]
    return jnp.split(m, N_MOD, axis=-1)

def modulate(x, w, shift, scale):
    return rmsnorm(x, w) * (1.0 + scale) + shift

def _rope_1d(x, ang):
    cos = jnp.cos(ang)
    sin = jnp.sin(ang)
    cos = jnp.concatenate([cos, cos], axis=-1).astype(x.dtype)
    sin = jnp.concatenate([sin, sin], axis=-1).astype(x.dtype)
    half = x.shape[-1] // 2
    rot = jnp.concatenate([-x[..., half:], x[..., :half]], axis=-1)
    return x * cos + rot * sin

def apply_axial_rope(t):
    seq_len = t.shape[1]
    n_rows = seq_len // GRID_W
    rows = jnp.repeat(jnp.arange(n_rows, dtype=jnp.float32), GRID_W)
    cols = jnp.tile(jnp.arange(GRID_W, dtype=jnp.float32), n_rows)
    axis_dim = ATT_HEAD_DIM // 2
    inv_freq = 1.0 / (ROPE_THETA ** (jnp.arange(0, axis_dim, 2, dtype=jnp.float32) / axis_dim))
    ang_r = (rows[:, None] * inv_freq)[:, None, None, :]
    ang_c = (cols[:, None] * inv_freq)[:, None, None, :]
    return jnp.concatenate([_rope_1d(t[..., :axis_dim], ang_r), _rope_1d(t[..., axis_dim:], ang_c)], axis=-1)

def pool_mixer(p, pool_w, pool_scale):
    bsz, seq_len, ch = p.shape
    pf = p.astype(jnp.float32)
    cs = jnp.concatenate([jnp.zeros((bsz, 1, ch), jnp.float32), jnp.cumsum(pf, axis=1)], axis=1)
    t = jnp.arange(seq_len)
    outs = []
    for g, win in enumerate(POOL_WINDOWS):
        lo = jnp.clip(t - win // 2, 0, seq_len)
        hi = jnp.clip(t + win // 2, 0, seq_len)
        sl = slice(g * POOL_GROUP_CH, (g + 1) * POOL_GROUP_CH)
        csg = cs[:, :, sl]
        mean = (csg[:, hi] - csg[:, lo]) / (hi - lo).astype(jnp.float32)[None, :, None]
        outs.append(mean - pf[:, :, sl])
    pooled = jnp.stack(outs, axis=2).astype(p.dtype)
    mixed = jnp.einsum("blgc,gcd->blgd", pooled, pool_w).reshape(bsz, seq_len, POOL_WIDTH)
    return mixed * pool_scale

def depthwise_conv_centred(u, w, b):
    ch, width = w.shape
    rhs = jnp.transpose(w)[:, None, :].astype(u.dtype)
    out = lax.conv_general_dilated(u, rhs, window_strides=(1,), padding=[(width // 2, width // 2)],
                                   dimension_numbers=("NWC", "WIO", "NWC"), feature_group_count=ch)
    return out + b

def ssd_chunked_scan(x, dt, a, b_in, c_in, d_skip, init_state):
    out_dtype = x.dtype
    f = jnp.float32
    bsz, seq_len = x.shape[:2]
    nc = seq_len // SSD_CHUNK
    rep = SSD_HEADS // SSD_GROUPS
    xc = x.astype(f).reshape(bsz, nc, SSD_CHUNK, SSD_HEADS, SSD_HEAD_DIM)
    dtc = dt.astype(f).reshape(bsz, nc, SSD_CHUNK, SSD_HEADS)
    bc = jnp.repeat(b_in.astype(f), rep, axis=2).reshape(bsz, nc, SSD_CHUNK, SSD_HEADS, SSD_STATE)
    cc = jnp.repeat(c_in.astype(f), rep, axis=2).reshape(bsz, nc, SSD_CHUNK, SSD_HEADS, SSD_STATE)
    a_cs = jnp.cumsum(dtc * a.astype(f), axis=2)
    mask = jnp.tril(jnp.ones((SSD_CHUNK, SSD_CHUNK), dtype=bool))[None, None, :, :, None]
    seg = a_cs[:, :, :, None, :] - a_cs[:, :, None, :, :]
    decay = jnp.exp(jnp.where(mask, seg, -jnp.inf))
    xdt = xc * dtc[..., None]
    scores = jnp.einsum("bcihn,bcjhn->bcijh", cc, bc) * decay
    y_diag = jnp.einsum("bcijh,bcjhp->bcihp", scores, xdt)
    decay_to_end = jnp.exp(a_cs[:, :, -1:, :] - a_cs)
    chunk_states = jnp.einsum("bcjhn,bcjh,bcjhp->bchpn", bc, decay_to_end, xdt)
    chunk_decay = jnp.exp(a_cs[:, :, -1, :])

    def step(state, inp):
        dec, st = inp
        return state * dec[:, :, None, None] + st, state

    final, entering = lax.scan(step, init_state.astype(f),
                               (jnp.moveaxis(chunk_decay, 1, 0), jnp.moveaxis(chunk_states, 1, 0)))
    entering = jnp.moveaxis(entering, 0, 1)
    y_off = jnp.einsum("bcihn,bchpn->bcihp", cc, entering) * jnp.exp(a_cs)[..., None]
    y = y_diag + y_off + xc * d_skip.astype(f)[:, None]
    return y.reshape(bsz, seq_len, SSD_HEADS, SSD_HEAD_DIM).astype(out_dtype), final.astype(out_dtype)

def ssd_mixer(z, xbc, dt_raw, lp, init_f, init_b):
    bsz, seq_len, _ = xbc.shape
    xbc = jax.nn.silu(depthwise_conv_centred(xbc, lp["ssd_conv_w"], lp["ssd_conv_b"]))
    xs, b_in, c_in = jnp.split(xbc, [SSD_WIDTH, SSD_WIDTH + SSD_GROUPS * SSD_STATE], axis=-1)
    xs = xs.reshape(bsz, seq_len, SSD_HEADS, SSD_HEAD_DIM)
    b_in = b_in.reshape(bsz, seq_len, SSD_GROUPS, SSD_STATE)
    c_in = c_in.reshape(bsz, seq_len, SSD_GROUPS, SSD_STATE)
    dt = jax.nn.softplus((dt_raw.reshape(bsz, seq_len, 2, SSD_HEADS) + lp["ssd_dt_bias"]).astype(jnp.float32))
    a = -jnp.exp(lp["ssd_A_log"].astype(jnp.float32))
    y_f, s_f = ssd_chunked_scan(xs, dt[:, :, 0], a[0], b_in, c_in, lp["ssd_D"][0], init_f)
    flip = lambda u: jnp.flip(u, axis=1)
    y_b, s_b = ssd_chunked_scan(flip(xs), flip(dt[:, :, 1]), a[1], flip(b_in), flip(c_in), lp["ssd_D"][1], init_b)
    y = (y_f + flip(y_b)).reshape(bsz, seq_len, SSD_WIDTH)
    y = rmsnorm(y * jax.nn.silu(z), lp["ssd_norm_w"])
    return y, s_f, s_b

def diff_attention(q, k, v, lam):
    bsz, seq_q = q.shape[:2]
    nb = seq_q // Q_BLOCK
    qb = q.reshape(bsz, nb, Q_BLOCK, ATT_HEADS, 2, ATT_HEAD_DIM).swapaxes(0, 1)
    scale = ATT_HEAD_DIM ** -0.5

    def block(qi):
        s = jnp.einsum("bqhmd,bkhmd->bmhqk", qi, k).astype(jnp.float32) * scale
        p = jax.nn.softmax(s, axis=-1)
        w = (p[:, 0] - lam * p[:, 1]).astype(v.dtype)
        return jnp.einsum("bhqk,bkhd->bqhd", w, v)

    o = lax.map(block, qb)
    return o.swapaxes(0, 1).reshape(bsz, seq_q, ATT_HEADS, ATT_V)

def peer_ffn(h, lp):
    bsz, seq_len, d = h.shape
    n_tok = bsz * seq_len
    xt = h.reshape(n_tok, d)
    q = (xt @ lp["peer_wq"]).reshape(n_tok, PEER_HEADS, 2, PEER_HALF)
    s = jnp.einsum("thmd,mhnd->thmn", q, lp["peer_keys"]).astype(jnp.float32)
    v1, i1 = lax.top_k(s[:, :, 0], PEER_TOPK)
    v2, i2 = lax.top_k(s[:, :, 1], PEER_TOPK)
    cand_s = (v1[..., :, None] + v2[..., None, :]).reshape(n_tok, PEER_HEADS, PEER_TOPK * PEER_TOPK)
    cand_i = (i1[..., :, None] * PEER_KEYS + i2[..., None, :]).reshape(n_tok, PEER_HEADS, PEER_TOPK * PEER_TOPK)
    top_s, pos = lax.top_k(cand_s, PEER_TOPK)
    idx = jnp.take_along_axis(cand_i, pos, axis=-1)
    g = jax.nn.softmax(top_s, axis=-1).astype(h.dtype)
    u_tab = lp["peer_u"]
    v_tab = lp["peer_v"]
    nb = n_tok // PEER_BLOCK

    def block(args):
        xb, ib, gb = args
        act = jnp.einsum("td,thkd->thk", xb, u_tab[ib])
        return jnp.einsum("thk,thkd->td", jax.nn.gelu(act) * gb, v_tab[ib])

    out = lax.map(block, (xt.reshape(nb, PEER_BLOCK, d),
                          idx.reshape(nb, PEER_BLOCK, PEER_HEADS, PEER_TOPK),
                          g.reshape(nb, PEER_BLOCK, PEER_HEADS, PEER_TOPK)))
    return out.reshape(bsz, seq_len, d)

def token_mixers(h, lp, layer_idx, ctx_k, ctx_v, init_f, init_b, latent):
    bsz, seq_len, _ = h.shape
    proj = h @ lp["w_in"]
    sizes = (POOL_WIDTH, SSD_WIDTH, SSD_CONV_CH, 2 * SSD_HEADS,
             ATT_HEADS * ATT_QK, ATT_HEADS * ATT_QK, ATT_HEADS * ATT_V)
    offsets = [int(o) for o in np.cumsum(sizes)[:-1]]
    p_in, z, xbc, dt_raw, q, k, v = jnp.split(proj, offsets, axis=-1)
    pool_out = pool_mixer(p_in, lp["pool_w"], lp["pool_scale"])
    ssd_out, s_f, s_b = ssd_mixer(z, xbc, dt_raw, lp, init_f, init_b)
    q = q.reshape(bsz, seq_len, ATT_HEADS, 2, ATT_HEAD_DIM)
    k = k.reshape(bsz, seq_len, ATT_HEADS, 2, ATT_HEAD_DIM)
    v = v.reshape(bsz, seq_len, ATT_HEADS, ATT_V)
    lam_init = 0.8 - 0.6 * math.exp(-0.3 * layer_idx)
    lq1, lk1, lq2, lk2 = lp["attn_lambda"].astype(jnp.float32)
    lam = jnp.exp(jnp.sum(lq1 * lk1)) - jnp.exp(jnp.sum(lq2 * lk2)) + lam_init
    if latent:
        q_att = apply_axial_rope(q)
        k_att = jnp.concatenate([apply_axial_rope(k), ctx_k.reshape(bsz, -1, ATT_HEADS, 2, ATT_HEAD_DIM)], axis=1)
        v_att = jnp.concatenate([v, ctx_v], axis=1)
    else:
        q_att, k_att, v_att = q, k, v
    o = diff_attention(q_att, k_att, v_att, lam)
    o = (rmsnorm(o, lp["attn_subln_w"]) * (1.0 - lam_init)).reshape(bsz, seq_len, ATT_WIDTH)
    out = jnp.concatenate([pool_out, ssd_out, o], axis=-1) @ lp["w_out"]
    return out, k.reshape(bsz, seq_len, ATT_HEADS, ATT_QK), v, s_f, s_b

def trunk_layer(x, cond, lp, layer_idx, ctx_k, ctx_v, init_f, init_b, latent):
    sh1, sc1, g1, sh2, sc2, g2 = adaln(cond, lp["mod_w"], lp["mod_b"])
    mix, k, v, s_f, s_b = token_mixers(modulate(x, lp["norm1_w"], sh1, sc1), lp, layer_idx,
                                       ctx_k, ctx_v, init_f, init_b, latent)
    x = x + g1 * mix
    x = x + g2 * peer_ffn(modulate(x, lp["norm2_w"], sh2, sc2), lp)
    return x, k, v, s_f, s_b

def setup_inputs(seed: int = 0) -> dict:
    key = jax.random.key(seed)
    ks = jax.random.split(key, 30)
    f32 = jnp.float32

    def nrm(kk, shape, scale):
        return jax.random.normal(kk, shape, f32) * scale

    dt0 = jnp.exp(jax.random.uniform(ks[18], (DEPTH, 2, SSD_HEADS), f32, math.log(1e-3), math.log(1e-1)))
    return {
        "x_prompt": nrm(ks[0], (BATCH, SEQ, D_MODEL), 1.0),
        "x_sample": nrm(ks[1], (DEC_BATCH, DEC_SEQ, D_MODEL), 1.0),
        "cache_attn_k": nrm(ks[2], (DEC_BATCH, DEPTH, PAST_LEN, ATT_HEADS, ATT_QK), 1.0),
        "cache_attn_v": nrm(ks[3], (DEC_BATCH, DEPTH, PAST_LEN, ATT_HEADS, ATT_V), 1.0),
        "state_ssd_fwd": nrm(ks[4], (DEC_BATCH, DEPTH, SSD_HEADS, SSD_HEAD_DIM, SSD_STATE), 0.5),
        "state_ssd_bwd": nrm(ks[5], (DEC_BATCH, DEPTH, SSD_HEADS, SSD_HEAD_DIM, SSD_STATE), 0.5),
        "c": nrm(ks[6], (DEC_BATCH, D_MODEL), 1.0),
        "c_ctx": nrm(ks[7], (D_MODEL,), 1.0),
        "mod_w": nrm(ks[8], (DEPTH, D_MODEL, N_MOD * D_MODEL), D_MODEL ** -0.5),
        "mod_b": nrm(ks[9], (DEPTH, N_MOD * D_MODEL), 0.02),
        "norm1_w": 1.0 + nrm(ks[10], (DEPTH, D_MODEL), 0.05),
        "norm2_w": 1.0 + nrm(ks[11], (DEPTH, D_MODEL), 0.05),
        "w_in": nrm(ks[12], (DEPTH, D_MODEL, IN_COLS), D_MODEL ** -0.5),
        "pool_w": nrm(ks[13], (DEPTH, POOL_GROUPS, POOL_GROUP_CH, POOL_GROUP_CH), POOL_GROUP_CH ** -0.5),
        "pool_scale": 1.0 + nrm(ks[14], (DEPTH, POOL_WIDTH), 0.05),
        "ssd_conv_w": nrm(ks[15], (DEPTH, SSD_CONV_CH, SSD_CONV), SSD_CONV ** -0.5),
        "ssd_conv_b": nrm(ks[16], (DEPTH, SSD_CONV_CH), 0.02),
        "ssd_A_log": jnp.log(jax.random.uniform(ks[17], (DEPTH, 2, SSD_HEADS), f32, 1.0, 16.0)),
        "ssd_dt_bias": dt0 + jnp.log(-jnp.expm1(-dt0)),
        "ssd_D": 1.0 + nrm(ks[19], (DEPTH, 2, SSD_HEADS), 0.05),
        "ssd_norm_w": 1.0 + nrm(ks[20], (DEPTH, SSD_WIDTH), 0.05),
        "attn_lambda": nrm(ks[21], (DEPTH, 4, ATT_HEAD_DIM), 0.1),
        "attn_subln_w": 1.0 + nrm(ks[22], (DEPTH, ATT_V), 0.05),
        "w_out": nrm(ks[23], (DEPTH, MIX_WIDTH, D_MODEL), MIX_WIDTH ** -0.5),
        "peer_wq": nrm(ks[24], (DEPTH, D_MODEL, PEER_HEADS * PEER_QDIM), D_MODEL ** -0.5),
        "peer_keys": nrm(ks[25], (DEPTH, 2, PEER_HEADS, PEER_KEYS, PEER_HALF), PEER_HALF ** -0.5),
        "peer_u": nrm(ks[26], (DEPTH, PEER_EXPERTS, D_MODEL), D_MODEL ** -0.5),
        "peer_v": nrm(ks[27], (DEPTH, PEER_EXPERTS, D_MODEL), PEER_HEADS ** -0.5),
        "final_norm_w": 1.0 + nrm(ks[28], (D_MODEL,), 0.05),
    }

def reference(x_prompt, x_sample, cache_attn_k, cache_attn_v, state_ssd_fwd, state_ssd_bwd, c, c_ctx,
              mod_w, mod_b, norm1_w, norm2_w, w_in, pool_w, pool_scale, ssd_conv_w, ssd_conv_b,
              ssd_A_log, ssd_dt_bias, ssd_D, ssd_norm_w, attn_lambda, attn_subln_w, w_out,
              peer_wq, peer_keys, peer_u, peer_v, final_norm_w):
    n_prompt = x_prompt.shape[0]
    zero_state = jnp.zeros((n_prompt, SSD_HEADS, SSD_HEAD_DIM, SSD_STATE), x_prompt.dtype)
    xp = x_prompt
    xs = x_sample
    ks_, vs_, sfs_, sbs_ = [], [], [], []
    for l in range(DEPTH):
        lp = {
            "mod_w": mod_w[l], "mod_b": mod_b[l], "norm1_w": norm1_w[l], "norm2_w": norm2_w[l],
            "w_in": w_in[l], "pool_w": pool_w[l], "pool_scale": pool_scale[l],
            "ssd_conv_w": ssd_conv_w[l], "ssd_conv_b": ssd_conv_b[l], "ssd_A_log": ssd_A_log[l],
            "ssd_dt_bias": ssd_dt_bias[l], "ssd_D": ssd_D[l], "ssd_norm_w": ssd_norm_w[l],
            "attn_lambda": attn_lambda[l], "attn_subln_w": attn_subln_w[l], "w_out": w_out[l],
            "peer_wq": peer_wq[l], "peer_keys": peer_keys[l], "peer_u": peer_u[l], "peer_v": peer_v[l],
        }
        xp, k_ctx, v_ctx, s_f, s_b = trunk_layer(xp, c_ctx, lp, l, None, None, zero_state, zero_state, False)
        ks_.append(k_ctx)
        vs_.append(v_ctx)
        sfs_.append(s_f)
        sbs_.append(s_b)
        xs, _, _, _, _ = trunk_layer(xs, c, lp, l, cache_attn_k[:, l], cache_attn_v[:, l],
                                     state_ssd_fwd[:, l], state_ssd_bwd[:, l], True)
    y_prompt = rmsnorm(xp, final_norm_w)
    y_sample = rmsnorm(xs, final_norm_w)
    new_attn_k = jnp.stack(ks_, axis=1)
    new_attn_v = jnp.stack(vs_, axis=1)
    new_ssd_fwd = jnp.stack(sfs_, axis=1)
    new_ssd_bwd = jnp.stack(sbs_, axis=1)
    return (y_prompt, y_sample, new_attn_k, new_attn_v, new_ssd_fwd, new_ssd_bwd)


_drawn_inputs = setup_inputs


def setup_inputs(seed=0):
    import zlib

    import numpy as np

    out = dict(_drawn_inputs(seed))
    spreads = {}
    factors = {}
    for name, (base, spread) in spreads.items():
        noise = np.random.default_rng([zlib.crc32(name.encode()), seed]).standard_normal(out[name].shape)
        drawn = base * np.exp(spread * noise) if base else spread * noise
        out[name] = jnp.asarray(drawn.astype(out[name].dtype))
    for name, factor in factors.items():
        out[name] = (out[name] * factor).astype(out[name].dtype)
    return out
```

```python
from contextlib import ExitStack

import numpy as np

import concourse.bass as bass
from concourse import mybir

ALU = mybir.AluOpType
ACT = mybir.ActivationFunctionType
F32 = mybir.dt.float32
U32 = mybir.dt.uint32
AX_X = mybir.AxisListType.X

P = 128
D = 1024
DB = D // P
DEPTH = 2
EPS = 1e-6
POOL_WINDOWS = (2, 4, 8, 16)
GRID_W = 64
SSD_HEADS = 4
CONV_BLOCKS = 6
TAPS = 5
ATT_HEADS = 4
ATT_SCALE = 64 ** -0.5
PEER_HEADS = 8
TOPK = 16
EXPERTS = 128 * 128
PICKS = PEER_HEADS * TOPK
CHUNK = 512
BANKS = 8
RING = 8
TURN = 16
NEG = -1e30
LOWEST = -3.0e38
STEPS = 2 * DEPTH
W_SLOTS = 2

W_IN = {"pz": (0, 512), "xb0": (512, 512), "xb1": (1024, 264), "q": (1288, 512), "k": (1800, 512), "v": (2312, 512)}


def shape_constants():
    j, i = np.arange(P)[:, None], np.arange(P)[None, :]
    parts = {
        "ident": (j == i).astype(np.float32),
        "tri": np.concatenate([(j <= i), (j >= i)], 1).astype(np.float32),
        "mask": np.concatenate([np.where(j <= i, 0.0, NEG), np.where(j >= i, 0.0, NEG)], 1),
        "ones": np.ones((P, P)),
        "iota": np.tile(np.arange(TOPK, dtype=np.float32), (P, 1)),
    }
    n = np.arange(2 * P)
    inv = 1.0 / (np.float32(10000.0) ** (np.arange(0, 32, 2, dtype=np.float32) / np.float32(32)))
    row = (n // GRID_W).astype(np.float32)[:, None] * inv.astype(np.float32)
    col = (n % GRID_W).astype(np.float32)[:, None] * inv.astype(np.float32)
    cos = np.concatenate([np.cos(row), np.cos(row), np.cos(col), np.cos(col)], 1)
    sin = np.concatenate([-np.sin(row), np.sin(row), -np.sin(col), np.sin(col)], 1)
    parts["cos"] = cos.reshape(2, P, 64).transpose(1, 0, 2).reshape(P, 128)
    parts["sin"] = sin.reshape(2, P, 64).transpose(1, 0, 2).reshape(P, 128)
    lam_init = [0.8 - 0.6 * float(np.exp(-0.3 * layer)) for layer in range(DEPTH)]
    parts["lam"] = np.tile(np.array([lam_init + [1.0 - x for x in lam_init]]), (P, 1))
    at, where = 0, {}
    for name, a in parts.items():
        where[name] = (at, a.shape[1])
        at += a.shape[1]
    bands = []
    for length in (2 * P, P):
        t = np.arange(length)
        for w in POOL_WINDOWS:
            lo, hi = np.clip(t - w // 2, 0, length), np.clip(t + w // 2, 0, length)
            b = ((t[:, None] >= lo) & (t[:, None] < hi)) / (hi - lo)[None, :] - np.eye(length)
            bands.append(b.reshape(length // P, P, length).transpose(1, 0, 2).reshape(P, -1))
    lat = np.concatenate(bands[:4], 1).astype(np.float32)
    ctx = np.concatenate(bands[4:], 1).astype(np.float32)
    return where, np.concatenate(list(parts.values()), 1).astype(np.float32), lat, ctx


class Marks:

    def __init__(self, sems, known):
        self.sems, self.known, self.reached, self.total = sems, known, {}, {}

    def mark(self, name, *key, n=1):
        self.total[name] = self.total.get(name, 0) + n
        self.reached[name, *key] = self.total[name]
        return self.sems[name], n

    def after(self, name, *key):
        if not self.known:
            return self.sems[name], 1
        return self.sems[name], self.known[name, *key]


EVENTS = """consts_in x_in cond_in cond_ready par_in par_ready bias_in nw_in row_stored
mod_a mod_b mod_g1 mod_g2 cache_in init_in band_in keys_in newk newv states_out fw_in y_out
ss h1 rope conv_sum conv dt_abs dt_exp dt_sum dt_ln dta nacs decays rep E M xw enter yo_done silu_z y_n
par_lam lam mx aw o_n h2 x_mid topk_diff topk_exp picked picks_copied act_done gelu weights x_new y_ready
pool_step act_step v_step sums o_done dots_copied""".split()


def build_pass(nc, io, where, known):
    jobs, events = known or ({}, {})
    stack = ExitStack()
    with stack:
        def sb(name, cols, dt=F32, rows=P):
            return stack.enter_context(nc.sbuf_tensor(name, [rows, cols], dt))

        sems = {n: stack.enter_context(nc.semaphore(n)) for n in EVENTS}
        for n in range(BANKS):
            sems["psum_full", n] = stack.enter_context(nc.semaphore(f"psum_full{n}"))
            sems["psum_taken", n] = stack.enter_context(nc.semaphore(f"psum_taken{n}"))
        w_landed = [stack.enter_context(nc.semaphore(f"w_landed{n}")) for n in range(W_SLOTS)]
        row_landed = [stack.enter_context(nc.semaphore(f"row_landed{n}")) for n in range(RING)]
        row_used = stack.enter_context(nc.semaphore("row_used"))
        row_go = stack.enter_context(nc.semaphore("row_go"))
        M = Marks(sems, events)
        mark, after = M.mark, M.after
        numbers = {}
        took = []

        x = [sb(f"x{t}", D) for t in range(3)]
        hn = [sb(f"hn{t}", D) for t in range(3)]
        mod_a, mod_b, mod_g1 = sb("mod_a", D), sb("mod_b", D), sb("mod_g1", D)
        mod_g2 = [sb(f"mod_g2{s}", D) for s in range(2)]
        wring = [sb(f"wring{n}", DB * CHUNK) for n in range(W_SLOTS)]
        rows = [sb(f"rows{n}", D) for n in range(RING)]
        acc = [sb(f"acc{n}", D) for n in range(2)]
        work = sb("work", 18220)
        mod_row, mod_bias, mod_nw = sb("mod_row", CHUNK), sb("mod_bias", CHUNK), sb("mod_nw", CHUNK)
        n_const = sum(n for _, n in where.values())
        const = sb("const", n_const)
        par = sb("par", 520)
        small = sb("small", 220)
        idx = sb("idx", 3 * PICKS, U32)
        idx_now = sb("idx_now", TURN, U32)
        gates = sb("gates", 3 * PICKS)
        dots = sb("dots", 3 * PICKS)
        dots_now = sb("dots_now", TURN)
        picks_w = sb("picks_w", 3 * PICKS)
        psum = [stack.enter_context(nc.psum_tensor(f"psum{n}", [P, CHUNK], F32)) for n in range(BANKS)]

        def c(name, a=0, n=None):
            at, size = where[name]
            return const[:, at + a:at + (size if n is None else a + n)]

        ident, ones = c("ident"), c("ones")
        tri = [c("tri", 0, P), c("tri", P, P)]
        mask = [c("mask", 0, P), c("mask", P, P)]

        def region(at, n):
            return work[:, at:at + n]

        qk = [region(t * 1024, 1024) for t in range(2)]
        catT = region(0, 2048).rearrange("p (b n) -> p b n", b=8)
        v_nat = [region(2048 + t * 512, 512) for t in range(2)]
        pz = [region(3072 + t * 512, 512) for t in range(2)]
        xraw = region(4096, 1560).rearrange("p (b n) -> p b n", b=6)
        decay = region(4096, 1024)
        conv = region(5656, 1536).rearrange("p (b n) -> p b n", b=6)
        nat = [region(7192 + t * 512, 512) for t in range(2)]
        qT = region(8216, 1024).rearrange("p (h n) -> p h n", h=4)
        kT = region(9240, 1536).rearrange("p (h n) -> p h n", h=4)
        hT = [region(10776, 2048).rearrange("p (b n) -> p b n", b=8),
              region(2048, 2048).rearrange("p (b n) -> p b n", b=8)]
        band = region(10776, 2048)
        prob = [[region(10776 + (2 * a + m) * 384, 384) for m in range(2)] for a in range(2)]
        wT = [region(12312 + a * 384, 384) for a in range(2)]
        k_cached, v_cached = region(13080, 512), region(13592, 512)
        rope_tmp = region(14104, 1024)
        mixed, xw, init_nat = region(14104, 512), region(14616, 512), region(15128, 512)
        enter0, enter1 = region(15640, 512), region(16152, 512)
        y_nat = [region(16664 + t * 256, 256) for t in range(2)]
        o_nat = region(17176, 512)
        pooledT = region(17688, 512).rearrange("p (b n) -> p b n", b=2)
        dta_rep = region(17176, 1024)
        pqT = region(4096, 4096).rearrange("p (b n) -> p b n", b=16)
        keys_nat, keysT = region(8216, 2048), region(10776, 2048)
        scores = region(12824, 2048)
        cand = region(14872, 2048)
        hot = [region(0, 2048), region(2048, 2048)]
        top_v = region(16920, 256)
        top_i = region(17176, 256).bitcast(U32)
        top_f = region(17432, 256)
        best_v = region(17688, 128)
        best_p = region(17816, 128).bitcast(U32)
        half_p = region(17944, 128).bitcast(U32)
        half_f = [region(18072, 128), small[:, 92:220]]
        dtraw = small[:, 0:16]
        ss = small[:, 16:20]
        rstd = small[:, 20:24]
        mx = [small[:, 24 + 2 * a:26 + 2 * a] for a in range(2)]
        sums = [small[:, 28 + 2 * a:30 + 2 * a] for a in range(2)]
        e_sum = small[:, 32:40]
        dot2 = small[:, 40:44]
        cumsum = small[:, 44:92]
        conv_w = par[:, 0:30].rearrange("p (b n) -> p b n", b=6)
        columns = par[:, 30:41]
        conv_b, y_w, pool_s, subln = par[:, 30:36], par[:, 36:38], par[:, 38:40], par[:, 40:41]
        dt_bias, a_log, d_skip = par[:, 42:50], par[:, 50:58], par[:, 58:66]
        d_sum, lam = par[:, 66:70], par[:, 70:71]
        subln_s = par[:, 71:72]
        pool_w = par[:, 72:200].rearrange("p (b n) -> p b n", b=2)
        lam_in = par[:, 200:456]
        dt = par[:, 456:472]
        dta = par[:, 472:488]
        dt_end = par[:, 488:504]
        dt_tmp = par[:, 504:520]
        cond = sb("cond", 16)
        cond3 = cond[:, :].rearrange("p (s b) -> p b s", s=2)
        par_rows = sb("par_rows", P)
        dt_u = sb("dt_u", 48)
        root, root_bits = sb("root", 8), sb("root_bits", 4, U32)

        def job(pe, *key):
            n = len(numbers)
            numbers[key] = n
            if n >= BANKS:
                pe.wait_ge(sems["psum_taken", n % BANKS], n // BANKS)
            return psum[n % BANKS]

        def number(key):
            return jobs.get(key, 0)

        def bank(*key):
            return psum[number(key) % BANKS]

        def made(*key):
            n = numbers.get(key, number(key))
            return sems["psum_full", n % BANKS], 1

        def full(*key):
            return sems["psum_full", number(key) % BANKS], number(key) // BANKS + 1

        def take(*key):
            took.append(key)
            return sems["psum_taken", number(key) % BANKS], 1

        def taken(*key):
            return sems["psum_taken", number(key) % BANKS], number(key) // BANKS + 1

        class Step:
            def __init__(self, k):
                self.k, self.layer, self.s = k, k // 2, k % 2
                self.lat = self.s == 0
                self.T = 2 - self.s
                self.X = 2 * self.s
                self.N = P * self.T
                self.NK = self.N + (P if self.lat else 0)

        steps = [Step(k) for k in range(STEPS)]

        chunks = []
        for st in steps:
            if st.lat:
                chunks += [(("mod", st.layer, j), ("mod", st.layer, j)) for j in range(12)]
            k, last = st.k, st.T - 1
            chunks += [(("q", k), ("q", k, last)), (("k", k), ("k", k, last)), (("v", k), ("v", k, last)),
                       (("pz", k), ("pz", k, last)), (("xb0", k), ("xb", k, 3)), (("xb1", k), ("dt", k, last))]
            chunks += [(("wo", k, cc), ("wo", k, last, cc)) for cc in range(2)]
            chunks += [(("wq", k, cc), ("pq", k, 4 * cc + 3)) for cc in range(4)]
        chunk_no = {key: n for n, (key, _) in enumerate(chunks)}

        def chunk(*key):
            return wring[chunk_no[key] % W_SLOTS][:, :].rearrange("p (b n) -> p b n", b=DB)

        def chunk_landed(*key):
            n = chunk_no[key]
            return w_landed[n % W_SLOTS], 16 * (n // W_SLOTS + 1)

        passes = [(st.k, v, t) for st in steps for v in range(2) for t in range(st.T)]
        pass_base = {key: n * PICKS for n, key in enumerate(passes)}

        block = stack.enter_context(nc.Block())

        @block.sync
        def _(sp):
            def load(dst, src, name, *key):
                sp.dma_start(dst, src).then_inc(*mark(name, *key, n=16))

            def load_chunk(*key):
                n = chunk_no[key]
                if n >= W_SLOTS:
                    sp.wait_ge(*full(*chunks[n - W_SLOTS][1]))
                kind = key[0]
                if kind == "mod":
                    src, width = io["mod_w"][key[1], :, key[2] * CHUNK:(key[2] + 1) * CHUNK], CHUNK
                elif kind == "wo":
                    src, width = io["w_out"][key[1] // 2, :, key[2] * CHUNK:(key[2] + 1) * CHUNK], CHUNK
                elif kind == "wq":
                    src, width = io["peer_wq"][key[1] // 2, :, key[2] * CHUNK:(key[2] + 1) * CHUNK], CHUNK
                else:
                    at, width = W_IN[kind]
                    src = io["w_in"][key[1] // 2, :, at:at + width]
                sp.dma_start(chunk(*key)[:, :, 0:width], src.rearrange("(b p) n -> p b n", p=P))\
                  .then_inc(w_landed[n % W_SLOTS], 16)

            def load_params(layer):
                if layer:
                    sp.wait_ge(*full("pm", 2 * layer - 1, 1))
                    sp.wait_ge(*taken("oT", 2 * layer - 1, 0))
                    sp.wait_ge(*taken("pm", 2 * layer - 1, 1))
                def row(dst, src, n):
                    load(dst, src.rearrange("(a n) -> a n", a=1).broadcast_to([P, n]), "par_in", layer)
                load(conv_w, io["ssd_conv_w"][layer].rearrange("(b p) n -> p b n", p=P), "par_in", layer)
                if layer == 0:
                    sp.wait_ge(*full("cond"))
                at = 0
                for name, n in (("ssd_conv_b", 6), ("ssd_norm_w", 2), ("pool_scale", 2), ("attn_subln_w", 1)):
                    load(par_rows[at:at + n, :], io[name][layer].rearrange("(b p) -> b p", p=P), "par_in", layer)
                    at += n
                row(dt_bias, io["ssd_dt_bias"][layer].rearrange("a b -> (a b)"), 8)
                row(a_log, io["ssd_A_log"][layer].rearrange("a b -> (a b)"), 8)
                row(d_skip, io["ssd_D"][layer].rearrange("a b -> (a b)"), 8)
                load(pool_w, io["pool_w"][layer].rearrange("(b g) c d -> (g c) b d", g=2), "par_in", layer)
                row(lam_in, io["attn_lambda"][layer].rearrange("a b -> (a b)"), 256)

            def modulation(layer):
                for j in range(13):
                    if j < 12:
                        load_chunk("mod", layer, j)
                        if j or layer:
                            sp.wait_ge(*full("mod", *((layer, j - 1) if j else (layer - 1, 11))))
                        load(mod_bias[0:1, :], io["mod_b"][layer:layer + 1, j * CHUNK:(j + 1) * CHUNK], "bias_in", layer, j)
                        if j // 2 in (1, 4):
                            w = io["norm1_w"] if j // 2 == 1 else io["norm2_w"]
                            if j != 2 or layer:
                                last = {2: (layer - 1, 9), 3: (layer, 2), 8: (layer, 3), 9: (layer, 8)}[j]
                                sp.wait_ge(*taken("mod", *last))
                            load(mod_nw[0:2, :], w[layer:layer + 1, (j % 2) * CHUNK:(j % 2 + 1) * CHUNK]
                                 .broadcast_to([2, CHUNK]), "nw_in", layer, j)
                    if j:
                        sp.wait_ge(*taken("mod", layer, j - 1))
                        sp.dma_start(io["mod_scratch"][layer, (j - 1) // 2, :, ((j - 1) % 2) * CHUNK:((j - 1) % 2 + 1) * CHUNK],
                                     mod_row[0:2, :]).then_inc(*mark("row_stored", layer, j - 1, n=16))

            def mod_vector(dst, st, vec, name):
                load(dst[:, :], io["mod_scratch"][st.layer, vec, st.s:st.s + 1, :].broadcast_to([P, D]), name, st.k, vec)

            def first_vectors(st):
                sp.wait_ge(*after("row_stored", st.layer, 11))
                if st.k:
                    sp.wait_ge(*after("h2", st.k - 1, steps[st.k - 1].T - 1))
                mod_vector(mod_a, st, 1, "mod_a")
                mod_vector(mod_b, st, 0, "mod_b")
                mod_vector(mod_g1, st, 2, "mod_g1")

            load(const[:, :], io["const"], "consts_in")
            for s, src in enumerate((io["c"][0], io["c_ctx"])):
                load(par_rows[8 * s:8 * s + 8, :], src.rearrange("(b p) -> b p", p=P), "cond_in")
            load_params(0)
            load(x[0][:, :], io["x_sample"][0, 0:P, :], "x_in")
            load(x[1][:, :], io["x_sample"][0, P:2 * P, :], "x_in")
            load(x[2][:, :], io["x_prompt"][0], "x_in")
            modulation(0)
            first_vectors(steps[0])
            for st in steps:
                k, layer = st.k, st.layer
                load_chunk("q", k)
                load_chunk("k", k)
                sp.wait_ge(*after("h1", k, st.T - 1))
                mod_vector(mod_a, st, 4, "mod_a")
                mod_vector(mod_b, st, 3, "mod_b")
                if k >= 2:
                    sp.wait_ge(*after("x_new", k - 2, st.T - 1))
                mod_vector(mod_g2[st.s], st, 5, "mod_g2")
                if st.lat:
                    load(k_cached, io["cache_attn_k"][0, layer].rearrange("n h d -> n (h d)"), "cache_in", layer)
                    load(v_cached, io["cache_attn_v"][0, layer].rearrange("n h d -> n (h d)"), "cache_in", layer)
                load_chunk("v", k)
                load_chunk("pz", k)
                if not st.lat:
                    sp.wait_ge(*taken("k", k, 0))
                    sp.dma_start(io["new_k"][0, layer].rearrange("n h d -> n (h d)"), qk[0][:, 512:1024])\
                      .then_inc(*mark("newk", layer, n=16))
                load_chunk("xb0", k)
                load_chunk("xb1", k)
                if not st.lat:
                    sp.wait_ge(*taken("v", k, 0))
                    sp.dma_start(io["new_v"][0, layer].rearrange("n h d -> n (h d)"), v_nat[0])\
                      .then_inc(*mark("newv", layer, n=16))
                sp.wait_ge(*full("dt", k, st.T - 1))
                load(band[:, 0:4 * st.T * st.N], io["band_lat" if st.lat else "band_ctx"], "band_in", k)
                load_chunk("wo", k, 0)
                load_chunk("wo", k, 1)
                if st.lat:
                    sp.wait_ge(*after("rope", k, 1))
                    for d, name in enumerate(("state_fwd", "state_bwd")):
                        load(init_nat[:, d * 256:(d + 1) * 256].rearrange("p (g n) -> p g n", g=2),
                             io[name][0, layer].rearrange("(g h) p n -> (h p) g n", g=2), "init_in", layer)
                else:
                    sp.wait_ge(*taken("st", k))
                    for d, name in enumerate(("new_f", "new_b")):
                        sp.dma_start(io[name][0, layer].rearrange("(g h) p n -> (h p) g n", g=2),
                                     enter0[:, d * 256:(d + 1) * 256].rearrange("p (g n) -> p g n", g=2))\
                          .then_inc(*mark("states_out", layer, n=16))
                sp.wait_ge(*full("s", k, st.T - 1, ATT_HEADS - 1, 1))
                load(keys_nat.rearrange("p (b n) -> p b n", b=16),
                     io["peer_keys"][layer].rearrange("m h n d -> n (m h) d"), "keys_in", k)
                load_chunk("wq", k, 0)
                load_chunk("wq", k, 1)
                if k % 2 == 0:
                    first_vectors(steps[k + 1])
                load_chunk("wq", k, 2)
                load_chunk("wq", k, 3)
                if k % 2 == 1 and k + 1 < STEPS:
                    load_params(layer + 1)
                    modulation(layer + 1)
                    first_vectors(steps[k + 1])
            for st in steps[-2:]:
                for t in range(st.T):
                    sp.wait_ge(*after("act_done", st.k, t))
                load(hn[st.X][:, :], io["final_norm_w"].rearrange("(a n) -> a n", a=1).broadcast_to([P, D]), "fw_in", st.k)
                for t in range(st.T):
                    sp.wait_ge(*after("y_ready", st.k, t))
                    dst = io["y_sample"][0, t * P:(t + 1) * P, :] if st.lat else io["y_prompt"][0]
                    sp.dma_start(dst, x[st.X + t][:, :]).then_inc(*mark("y_out", st.k, t, n=16))
            sp.wait_ge(*after("y_out", STEPS - 1, 0))
            sp.wait_ge(*after("newk", DEPTH - 1))
            sp.wait_ge(*after("newv", DEPTH - 1))
            sp.wait_ge(*after("states_out", DEPTH - 1))

        @block.gpsimd
        def _(pool):
            tables = [io["peer_u"], io["peer_v"]]
            half = TURN // 2
            for n, (k, which, t) in enumerate(passes):
                if which == 0 and t == 0:
                    pass
                if which == 0:
                    pool.wait_ge(*after("picked", k, t))
                base, col = pass_base[k, which, t], (steps[k].X + t) * PICKS
                with pool.Fori(0, PICKS // TURN) as turn:
                    for part in range(2):
                        q = turn * TURN + (base + part * half)
                        pool.wait_ge(row_used, q + 1)
                        pool.sem_inc(row_go, 1)
                        nc.gpsimd.tensor_copy(idx_now[:, part * half:(part + 1) * half],
                                              idx[:, bass.ds(turn * TURN + (col + part * half), half)])\
                            .then_inc(sems["picks_copied"], 1)
                        pool.wait_ge(sems["picks_copied"], turn * 2 + (n * 2 * (PICKS // TURN) + part + 1))
                        for r in range(half):
                            if r % 2 == 0:
                                pool.wait_ge(row_used, q + (r + 2))
                                pool.sem_inc(row_go, 1)
                            nc.gpsimd.indirect_dma_start(
                                rows[r][:, :], None, tables[which],
                                bass.IndirectOffsetOnAxis(ap=idx_now[:, part * half + r:part * half + r + 1], axis=0))\
                                .then_inc(row_landed[r], 16)

        @block.tensor
        def _(pe):
            mm, tr = nc.tensor.matmul, nc.tensor.transpose

            def modulation(layer):
                if layer == 0:
                    pe.wait_ge(*after("consts_in"))
                    pe.wait_ge(*after("cond_in"))
                    p = job(pe, "cond")
                    tr(p[:, 0:16], par_rows[0:16, :], ident[0:16, 0:16]).then_inc(*made("cond"))
                    pe.wait_ge(*taken("cond"))
                for j in range(12):
                    p = job(pe, "mod", layer, j)
                    pe.wait_ge(*chunk_landed("mod", layer, j))
                    w = chunk("mod", layer, j)
                    for b in range(DB):
                        mm(p[0:2, :], cond3[:, b, :], w[:, b, :], start=(b == 0), stop=False)
                    pe.wait_ge(*after("bias_in", layer, j))
                    mm(p[0:2, :], ones[0:1, 0:2], mod_bias[0:1, :], start=False, stop=True)\
                        .then_inc(*made("mod", layer, j))

            def turn_h(st, which):
                name = ("hT1", "hT2")[which]
                for t in range(st.T):
                    pe.wait_ge(*after(("h1", "h2")[which], st.k, t))
                    for half in range(2):
                        p = job(pe, name, st.k, t, half)
                        for i in range(4):
                            b = 4 * half + i
                            ins = tr(p[:, i * P:(i + 1) * P], hn[st.X + t][:, b * P:(b + 1) * P], ident)
                        ins.then_inc(*made(name, st.k, t, half))

            def project(st, name, n, slot=0, key=None):
                k = st.k
                key = key or (name, k)
                pe.wait_ge(*chunk_landed(*key))
                w = chunk(*key)
                for t in range(st.T):
                    jk = (name, k, t)
                    p = job(pe, *jk)
                    for b in range(DB):
                        ins = mm(p[:, 0:n], hT[0][:, b, t * P:(t + 1) * P], w[:, b, slot:slot + n],
                                 start=(b == 0), stop=(b == DB - 1))
                    ins.then_inc(*made(*jk))

            def conv_project(st, blocks, key):
                pe.wait_ge(*chunk_landed(*key))
                w = chunk(*key)
                for i, bb in enumerate(blocks):
                    p = job(pe, "xb", st.k, bb)
                    for b in range(DB):
                        ins = mm(p[:, 0:st.N], w[:, b, i * P:(i + 1) * P], hT[0][:, b, 0:st.N],
                                 start=(b == 0), stop=(b == DB - 1))
                    ins.then_inc(*made("xb", st.k, bb))

            def dense(st):
                k, T, N = st.k, st.T, st.N
                if st.lat:
                    p = job(pe, "par", st.layer)
                    pe.wait_ge(*after("par_in", st.layer))
                    tr(p[:, 0:11], par_rows[0:11, :], ident[0:11, 0:11]).then_inc(*made("par", st.layer))
                turn_h(st, 0)
                pe.wait_ge(*taken("hT1", k, T - 1, 1))
                project(st, "q", CHUNK)
                project(st, "k", CHUNK)
                project(st, "v", CHUNK)
                project(st, "pz", CHUNK)
                conv_project(st, range(4), ("xb0", k))
                conv_project(st, range(4, 6), ("xb1", k))
                project(st, "dt", 8, slot=256, key=("xb1", k))
                for t in range(T):
                    if st.lat:
                        pe.wait_ge(*after("rope", k, t))
                    else:
                        pe.wait_ge(*taken("k", k, t))
                    for side in range(2):
                        p = job(pe, "qkT", k, t, side)
                        for h in range(4):
                            at = side * 512 + h * P
                            ins = tr(p[:, h * P:(h + 1) * P], qk[t][:, at:at + P], ident)
                        ins.then_inc(*made("qkT", k, t, side))
                if st.lat:
                    p = job(pe, "kc", k)
                    pe.wait_ge(*after("cache_in", st.layer))
                    for h in range(4):
                        ins = tr(p[:, h * P:(h + 1) * P], k_cached[:, h * P:(h + 1) * P], ident)
                    ins.then_inc(*made("kc", k))
                pe.wait_ge(*after("band_in", k))
                for pair in range(2):
                    p = job(pe, "pl", k, pair)
                    for r in range(2):
                        g = 2 * pair + r
                        for ti in range(T):
                            ins = mm(p[64 * r:64 * r + 64, 0:N], pz[ti][:, g * 64:(g + 1) * 64],
                                     band[:, (g * T + ti) * N:(g * T + ti + 1) * N], start=(ti == 0), stop=(ti == T - 1))
                    ins.then_inc(*made("pl", k, pair))
                for pair in range(2):
                    p = job(pe, "pm", k, pair)
                    pe.wait_ge(*taken("pl", k, pair))
                    for r in range(2):
                        ins = mm(p[64 * r:64 * r + 64, 0:N], pool_w[64 * r:64 * r + 64, pair, :],
                                 pooledT[64 * r:64 * r + 64, pair, 0:N], start=True, stop=True)
                    ins.then_inc(*made("pm", k, pair))
                p = job(pe, "cum", k)
                pe.wait_ge(*after("dta", k))
                for t in range(T):
                    o = 24 * t
                    mm(p[:, o:o + 4], tri[0], dta[:, 8 * t:8 * t + 4], start=True, stop=True)
                    mm(p[:, o + 4:o + 8], tri[1], dta[:, 8 * t + 4:8 * t + 8], start=True, stop=True)
                    ins = mm(p[:, o + 8:o + 16], ones, dta[:, 8 * t:8 * t + 8], start=True, stop=True)
                ins.then_inc(*made("cum", k))
                pe.wait_ge(*after("conv", k))
                for t in range(T):
                    p = job(pe, "xbn", k, t)
                    for b in range(4):
                        ins = tr(p[:, b * P:(b + 1) * P], conv[:, b, t * P:(t + 1) * P], ident)
                    ins.then_inc(*made("xbn", k, t))
                if st.lat:
                    p = job(pe, "init", k)
                    pe.wait_ge(*after("init_in", st.layer))
                    for b in range(4):
                        ins = tr(p[:, b * P:(b + 1) * P], init_nat[:, b * P:(b + 1) * P], ident)
                    ins.then_inc(*made("init", k))
                p = job(pe, "st", k)
                for d in range(2):
                    t = d if st.lat else 0
                    pe.wait_ge(*after("xw", k, d))
                    for g in range(2):
                        o = d * 256 + g * P
                        b_nat = nat[t][:, 256 + g * P:256 + (g + 1) * P]
                        x_w = xw[:, o:o + P]
                        ins = mm(p[:, o:o + P], *((b_nat, x_w) if st.lat else (x_w, b_nat)), start=True, stop=True)
                ins.then_inc(*made("st", k))
                for t in range(T):
                    p = job(pe, "cb", k, t)
                    for g in range(2):
                        ins = mm(p[:, g * P:(g + 1) * P], conv[:, 2 + g, t * P:(t + 1) * P],
                                 conv[:, 4 + g, t * P:(t + 1) * P], start=True, stop=True)
                    ins.then_inc(*made("cb", k, t))
                    pe.wait_ge(*after("rep", k, t))
                    for d in range(2):
                        p = job(pe, "seg", k, t, d)
                        mm(p[:, :].rearrange("p (h n) -> p h n", h=4), ident,
                           mask[d].unsqueeze(1).broadcast_to([P, 4, P]), start=True, stop=False)
                        for h in range(4):
                            ins = mm(p[:, h * P:(h + 1) * P], dta_rep[:, (4 * d + h) * P:(4 * d + h + 1) * P], tri[d],
                                     start=False, stop=(h == 3))
                        ins.then_inc(*made("seg", k, t, d))
                    if st.lat:
                        p = job(pe, "yo", k, t)
                        pe.wait_ge(*taken("init", k))
                        pe.wait_ge(*taken("st", k))
                        for d in range(2):
                            state = enter0 if d == t else enter1
                            for g in range(2):
                                o = d * 256 + g * P
                                ins = mm(p[:, o:o + P], conv[:, 4 + g, t * P:(t + 1) * P], state[:, o:o + P],
                                         start=True, stop=True)
                        ins.then_inc(*made("yo", k, t))
                    p = job(pe, "y", k, t)
                    pe.wait_ge(*after("M", k, t))
                    for h in range(4):
                        ins = mm(p[:, h * 64:(h + 1) * 64], mixed[:, h * P:(h + 1) * P], nat[t][:, h * 64:(h + 1) * 64],
                                 start=True, stop=True)
                    ins.then_inc(*made("y", k, t))
                for t in range(T):
                    p = job(pe, "yT", k, t)
                    pe.wait_ge(*after("y_n", k, t))
                    for b in range(2):
                        ins = tr(p[:, b * P:(b + 1) * P], y_nat[t][:, b * P:(b + 1) * P], ident)
                    ins.then_inc(*made("yT", k, t))
                heads = [(t, h) for t in range(T) for h in range(ATT_HEADS)]

                def scores_of(t, h):
                    for m in range(2):
                        p = job(pe, "s", k, t, h, m)
                        mm(p[:, 0:st.NK], qT[64 * m:64 * m + 64, h, t * P:(t + 1) * P], kT[64 * m:64 * m + 64, h, 0:st.NK],
                           start=True, stop=True).then_inc(*made("s", k, t, h, m))

                scores_of(*heads[0])
                for i, (t, h) in enumerate(heads):
                    if i + 1 < len(heads):
                        scores_of(*heads[i + 1])
                    p = job(pe, "wT", k, t, h)
                    pe.wait_ge(*after("aw", k, t, h))
                    for kt in range(st.NK // P):
                        ins = tr(p[:, kt * P:(kt + 1) * P], prob[i % 2][0][:, kt * P:(kt + 1) * P], ident)
                    ins.then_inc(*made("wT", k, t, h))
                    p = job(pe, "o", k, t, h)
                    pe.wait_ge(*taken("wT", k, t, h))
                    for kt in range(st.NK // P):
                        v = v_nat[kt] if kt < T else v_cached
                        ins = mm(p[:, 0:P], wT[i % 2][:, kt * P:(kt + 1) * P], v[:, h * P:(h + 1) * P],
                                 start=(kt == 0), stop=(kt == st.NK // P - 1))
                    ins.then_inc(*made("o", k, t, h))
                    if h == ATT_HEADS - 1:
                        p = job(pe, "oT", k, t)
                        pe.wait_ge(*after("o_n", k, t))
                        for b in range(4):
                            ins = tr(p[:, b * P:(b + 1) * P], o_nat[:, b * P:(b + 1) * P], ident)
                        ins.then_inc(*made("oT", k, t))
                pe.wait_ge(*taken("oT", k, T - 1))
                for cc in range(2):
                    pe.wait_ge(*chunk_landed("wo", k, cc))
                    for t in range(T):
                        p = job(pe, "wo", k, t, cc)
                        for b in range(DB):
                            ins = mm(p[:, :], catT[:, b, t * P:(t + 1) * P], chunk("wo", k, cc)[:, b, :],
                                     start=(b == 0), stop=(b == DB - 1))
                        ins.then_inc(*made("wo", k, t, cc))
                pe.wait_ge(*after("keys_in", k))
                for i in range(4):
                    p = job(pe, "kt", k, i)
                    for j in range(4):
                        b = 4 * i + j
                        ins = tr(p[:, j * P:(j + 1) * P], keys_nat[:, b * P:(b + 1) * P], ident)
                    ins.then_inc(*made("kt", k, i))
                turn_h(st, 1)
                pe.wait_ge(*taken("hT2", k, T - 1, 1))
                for b in range(16):
                    p = job(pe, "pq", k, b)
                    if b % 4 == 0:
                        pe.wait_ge(*chunk_landed("wq", k, b // 4))
                    for kb in range(DB):
                        ins = mm(p[:, 0:N], chunk("wq", k, b // 4)[:, kb, (b % 4) * P:(b % 4 + 1) * P], hT[1][:, kb, 0:N],
                                 start=(kb == 0), stop=(kb == DB - 1))
                    ins.then_inc(*made("pq", k, b))
                pe.wait_ge(*taken("pq", k, 15))
                for t in range(T):
                    for i in range(4):
                        p = job(pe, "ps", k, t, i)
                        for j in range(4):
                            b = 4 * i + j
                            key = (b % 2) * PEER_HEADS + b // 2
                            ins = mm(p[:, j * P:(j + 1) * P], pqT[:, b, t * P:(t + 1) * P], keysT[:, key * P:(key + 1) * P],
                                     start=True, stop=True)
                        ins.then_inc(*made("ps", k, t, i))

            for st in steps:
                if st.lat:
                    modulation(st.layer)
                dense(st)

        @block.scalar
        def _(act):
            A = nc.scalar.activation

            def modulation(layer):
                for j in range(12):
                    if j // 2 not in (1, 4):
                        act.wait_ge(*full("mod", layer, j))
                        if j or layer:
                            act.wait_ge(*after("row_stored", *((layer, j - 1) if j else (layer - 1, 11))))
                        A(mod_row[0:2, :], bank("mod", layer, j)[0:2, :], ACT.Copy).then_inc(*take("mod", layer, j))
                    yield ("mod", j)

            def carry(dst, src, *key, scale=1.0):
                act.wait_ge(*full(*key))
                A(dst, src, ACT.Copy, scale=scale).then_inc(*take(*key))

            def square(st, which):
                for t in range(st.T):
                    if which == 0:
                        if st.k < 2:
                            act.wait_ge(*after("x_in"))
                        else:
                            act.wait_ge(*after("x_new", st.k - 2, t))
                    else:
                        act.wait_ge(*after("x_mid", st.k, t))
                    A(hn[st.X + t][:, :], x[st.X + t][:, :], ACT.Square, accum_out=ss[:, t:t + 1])\
                        .then_inc(*mark("ss", st.k, which, t))

            def turn_h(st, which):
                name = ("hT1", "hT2")[which]
                for t in range(st.T):
                    for half in range(2):
                        carry(hT[which][:, 4 * half:4 * half + 4, t * P:(t + 1) * P],
                              bank(name, st.k, t, half)[:, :].rearrange("p (b n) -> p b n", b=4), name, st.k, t, half)

            def dense(st):
                k, T, N = st.k, st.T, st.N
                square(st, 0)
                yield "start"
                if st.lat:
                    carry(columns, bank("par", st.layer)[:, 0:11], "par", st.layer)
                turn_h(st, 0)
                for name, where_to in (("q", 0), ("k", 512)):
                    for t in range(T):
                        carry(qk[t][:, where_to:where_to + 512], bank(name, k, t)[:, :], name, k, t)
                for t in range(T):
                    carry(v_nat[t], bank("v", k, t)[:, :], "v", k, t)
                for t in range(T):
                    carry(pz[t], bank("pz", k, t)[:, :], "pz", k, t)
                for b in range(CONV_BLOCKS):
                    carry(xraw[:, b, 2:2 + N], bank("xb", k, b)[:, 0:N], "xb", k, b)
                for t in range(T):
                    carry(dtraw[:, 8 * t:8 * t + 8], bank("dt", k, t)[:, 0:8], "dt", k, t)
                if st.lat:
                    act.wait_ge(*after("par_in", st.layer))
                    A(a_log, a_log, ACT.Exp).then_inc(*mark("par_ready", st.layer))
                    act.wait_ge(*after("par_lam", st.layer))
                    A(dot2[:, 0:2], dot2[:, 0:2], ACT.Exp).then_inc(*mark("lam", st.layer))
                yield "rope"
                for t in range(T):
                    for side, dst in enumerate((qT, kT)):
                        carry(dst[:, :, t * P:(t + 1) * P],
                              bank("qkT", k, t, side)[:, :].rearrange("p (h n) -> p h n", h=4), "qkT", k, t, side)
                if st.lat:
                    carry(kT[:, :, N:N + P], bank("kc", k)[:, :].rearrange("p (h n) -> p h n", h=4), "kc", k)
                yield "conv"
                for pair in range(2):
                    carry(pooledT[:, pair, 0:N], bank("pl", k, pair)[:, 0:N], "pl", k, pair)
                if st.lat:
                    act.wait_ge(*after("par_in", st.layer))
                if not st.lat:
                    act.wait_ge(*after("newk", st.layer))
                for pair in range(2):
                    carry(catT[:, pair, 0:N], bank("pm", k, pair)[:, 0:N], "pm", k, pair, scale=pool_s[:, pair:pair + 1])
                act.wait_ge(*after("dt_abs", k))
                A(dt_u[:, 0:8 * T], dt_u[:, 0:8 * T], ACT.Exp, scale=-1.0).then_inc(*mark("dt_exp", k))
                act.wait_ge(*after("dt_sum", k))
                A(dt_u[:, 32:32 + 8 * T], dt_u[:, 16:16 + 8 * T], ACT.Ln).then_inc(*mark("dt_ln", k))
                act.wait_ge(*after("nacs", k))
                A(cumsum[:, 0:24 * T], cumsum[:, 0:24 * T], ACT.Exp).then_inc(*mark("decays", k))
                yield "dt"
                act.wait_ge(*after("conv_sum", k))
                A(conv[:, :, 0:N], conv[:, :, 0:N], ACT.Silu).then_inc(*mark("conv", k))
                for t in range(T):
                    A(pz[t][:, 256:512], pz[t][:, 256:512], ACT.Silu).then_inc(*mark("silu_z", k, t))
                for t in range(T):
                    carry(nat[t], bank("xbn", k, t)[:, :], "xbn", k, t)
                if st.lat:
                    carry(enter0, bank("init", k)[:, :], "init", k)
                yield "xw"
                if not st.lat:
                    carry(enter0, bank("st", k)[:, :], "st", k)
                for t in range(T):
                    for d in range(2):
                        act.wait_ge(*full("seg", k, t, d))
                        if d == 0 and t:
                            act.wait_ge(*after("M", k, t - 1))
                        for h in range(4):
                            o = (4 * d + h) * P
                            ins = A(decay[:, o:o + P], bank("seg", k, t, d)[:, h * P:(h + 1) * P], ACT.Exp,
                                    bias=dt_end[:, 8 * t + 4 * d + h:8 * t + 4 * d + h + 1])
                        ins.then_inc(*take("seg", k, t, d))
                    yield ("seg", t)
                for t in range(T):
                    for b in range(2):
                        act.wait_ge(*full("yT", k, t))
                        ins = A(catT[:, 2 + b, t * P:(t + 1) * P], bank("yT", k, t)[:, b * P:(b + 1) * P], ACT.Copy,
                                scale=y_w[:, b:b + 1])
                    ins.then_inc(*take("yT", k, t))
                yield "y"
                heads = [(t, h) for t in range(T) for h in range(ATT_HEADS)]

                def exps(i):
                    t, h = heads[i]
                    act.wait_ge(*after("mx", k, t, h))
                    for m in range(2):
                        A(prob[i % 2][m][:, 0:st.NK], bank("s", k, t, h, m)[:, 0:st.NK], ACT.Exp,
                          bias=mx[i % 2][:, m:m + 1], scale=ATT_SCALE,
                          accum_out=sums[i % 2][:, m:m + 1]).then_inc(*take("s", k, t, h, m))

                exps(0)
                for i, (t, h) in enumerate(heads):
                    if i + 1 < len(heads):
                        exps(i + 1)
                    carry(wT[i % 2][:, 0:st.NK], bank("wT", k, t, h)[:, 0:st.NK], "wT", k, t, h)
                    if h == 0 and t:
                        act.wait_ge(*full("oT", k, t - 1))
                    carry(o_nat[:, h * P:(h + 1) * P], bank("o", k, t, h)[:, 0:P], "o", k, t, h)
                    if h == ATT_HEADS - 1:
                        act.wait_ge(*full("oT", k, t))
                        A(catT[:, 4:8, t * P:(t + 1) * P], bank("oT", k, t)[:, :].rearrange("p (b n) -> p b n", b=4),
                          ACT.Copy, scale=subln_s).then_inc(*take("oT", k, t))
                    if h % 2 == 1:
                        yield ("att", 4 * t + h)
                for i in range(4):
                    carry(keysT[:, i * 512:(i + 1) * 512], bank("kt", k, i)[:, :], "kt", k, i)
                square(st, 1)
                yield "mid"
                turn_h(st, 1)
                for b in range(16):
                    carry(pqT[:, b, 0:N], bank("pq", k, b)[:, 0:N], "pq", k, b)
                for t in range(T):
                    for i in range(4):
                        if t and i == 0:
                            act.wait_ge(*after("picked", k, t - 1))
                        carry(scores[:, i * 512:(i + 1) * 512], bank("ps", k, t, i)[:, :], "ps", k, t, i)
                    yield ("ps", t)
                    act.wait_ge(*after("topk_diff", k, t))
                    A(best_v, best_v, ACT.Exp).then_inc(*mark("topk_exp", k, t))
                    yield ("exp", t)

            def gelu(k, t):
                at = (steps[k].X + t) * PICKS
                act.wait_ge(*after("act_done", k, t))
                A(dots[:, at:at + PICKS], dots[:, at:at + PICKS], ACT.Gelu_apprx_tanh).then_inc(*mark("gelu", k, t))

            act.wait_ge(*full("cond"))
            A(cond[:, :], bank("cond")[:, 0:16], ACT.Silu).then_inc(*take("cond"))
            run_beside(steps, modulation, dense, lambda k, kind, t, span: gelu(k, t) if kind == 2 else None, False)

        @block.vector
        def _(dve):
            V = nc.vector
            done = [0]

            def d(ins):
                done[0] += 1
                ins.then_inc(sems["v_step"], 1)

            def settle():
                dve.wait_ge(sems["v_step"], done[0])

            def inverse_rms(out, sq, n):
                w = out.shape[1]
                mean, by = root[:, 0:w], root[:, 4:4 + w]
                d(V.tensor_scalar(mean, sq, 1.0 / n, EPS, ALU.mult, ALU.add))
                settle()
                d(V.tensor_single_scalar(root_bits[:, 0:w], mean.bitcast(U32), 1, ALU.logical_shift_right))
                settle()
                d(V.tensor_scalar(out.bitcast(U32), root_bits[:, 0:w], -1.0, float(0x5F3759DF), ALU.mult, ALU.add))
                settle()
                for _ in range(4):
                    if w == 1:
                        d(V.scalar_tensor_tensor(by, out, mean, out, ALU.mult, ALU.mult))
                    else:
                        d(V.tensor_tensor(by, out, out, ALU.mult))
                        settle()
                        d(V.tensor_tensor(by, by, mean, ALU.mult))
                    settle()
                    d(V.tensor_scalar(by, by, -0.5, 1.5, ALU.mult, ALU.add))
                    settle()
                    d(V.tensor_tensor(out, out, by, ALU.mult))
                    settle()

            def modulation(layer):
                for j in range(12):
                    if j // 2 in (1, 4):
                        dve.wait_ge(*full("mod", layer, j))
                        dve.wait_ge(*after("nw_in", layer, j))
                        dve.wait_ge(*after("row_stored", layer, j - 1))
                        V.scalar_tensor_tensor(mod_row[0:2, :], bank("mod", layer, j)[0:2, :], 1.0, mod_nw[0:2, :],
                                               ALU.add, ALU.mult).then_inc(*take("mod", layer, j))
                    yield ("mod", j)

            def modulate(st, which):
                name = ("h1", "h2")[which]
                for t in range(st.T):
                    dve.wait_ge(*after("ss", st.k, which, t))
                    inverse_rms(rstd[:, t:t + 1], ss[:, t:t + 1], D)
                    h = hn[st.X + t][:, :]
                    dve.wait_ge(*after("mod_a", st.k, 4 if which else 1))
                    d(V.scalar_tensor_tensor(h, x[st.X + t][:, :], rstd[:, t:t + 1], mod_a[:, :], ALU.mult, ALU.mult))
                    settle()
                    dve.wait_ge(*after("mod_b", st.k, 3 if which else 0))
                    V.tensor_tensor(h, h, mod_b[:, :], ALU.add).then_inc(*mark(name, st.k, t))

            def rounds(values, n, width, top, index, t, at):
                for r in range(2):
                    for b in range(n):
                        d(V.max(top[:, b * TOPK + 8 * r:b * TOPK + 8 * r + 8], values[:, b * width:(b + 1) * width]))
                    settle()
                    for b in range(n):
                        d(V.max_index(index[:, b * TOPK + 8 * r:b * TOPK + 8 * r + 8],
                                      top[:, b * TOPK + 8 * r:b * TOPK + 8 * r + 8], values[:, b * width:(b + 1) * width]))
                    settle()
                    if r == 0:
                        for b in range(n):
                            d(V.match_replace(values[:, b * width:(b + 1) * width], top[:, b * TOPK:b * TOPK + 8],
                                              values[:, b * width:(b + 1) * width], LOWEST))
                        settle()
                    yield ("choose", t, at + r)

            def choose(st, t):
                k = st.k
                for i in range(4):
                    dve.wait_ge(*taken("ps", k, t, i))
                yield from rounds(scores, 2 * PEER_HEADS, P, top_v, top_i, t, 0)
                d(V.tensor_copy(top_f, top_i))
                tv = top_v.rearrange("p (h m a) -> p h m a", h=PEER_HEADS, m=2)
                d(V.tensor_tensor(cand.rearrange("p (h a b) -> p h a b", h=PEER_HEADS, a=TOPK),
                                  tv[:, :, 0, :].unsqueeze(3).broadcast_to([P, PEER_HEADS, TOPK, TOPK]),
                                  tv[:, :, 1, :].unsqueeze(2).broadcast_to([P, PEER_HEADS, TOPK, TOPK]), ALU.add))
                settle()
                yield from rounds(cand, PEER_HEADS, TOPK * TOPK, best_v, best_p, t, 2)
                d(V.tensor_single_scalar(half_p, best_p, 4, ALU.logical_shift_right))
                settle()
                d(V.tensor_copy(half_f[0], half_p))
                settle()
                d(V.tensor_single_scalar(half_p, best_p, 15, ALU.bitwise_and))
                settle()
                d(V.tensor_copy(half_f[1], half_p))
                settle()
                tf = top_f.rearrange("p (h m a) -> p h m a", h=PEER_HEADS, m=2)
                wide = [P, PEER_HEADS, TOPK, TOPK]
                for m in range(2):
                    hm = hot[m].rearrange("p (h k a) -> p h k a", h=PEER_HEADS, k=TOPK)
                    rank = half_f[m].rearrange("p (h k) -> p h k", h=PEER_HEADS).unsqueeze(3).broadcast_to(wide)
                    iota = c("iota").unsqueeze(1).unsqueeze(1).broadcast_to(wide)
                    d(V.tensor_tensor(hm, rank, iota, ALU.is_equal))
                    yield ("choose", t, 4 + m)
                settle()
                for m in range(2):
                    hm = hot[m].rearrange("p (h k a) -> p h k a", h=PEER_HEADS, k=TOPK)
                    d(V.tensor_tensor(hm, hm, tf[:, :, m, :].unsqueeze(2).broadcast_to(wide), ALU.mult))
                settle()
                yield ("choose", t, 6)
                for m in range(2):
                    d(V.tensor_reduce(half_f[m], hot[m].rearrange("p (q a) -> p q a", a=TOPK), AX_X, ALU.add))
                settle()
                at = (st.X + t) * PICKS
                d(V.tensor_scalar(half_f[0], half_f[0], float(P), float(st.layer * EXPERTS), ALU.mult, ALU.add))
                settle()
                d(V.tensor_tensor(idx[:, at:at + PICKS], half_f[0], half_f[1], ALU.add))
                bv = best_v.rearrange("p (h k) -> p h k", h=PEER_HEADS)
                d(V.tensor_copy(e_sum, bv[:, :, 0]))
                settle()
                V.tensor_tensor(bv, bv, e_sum.unsqueeze(2).broadcast_to([P, PEER_HEADS, TOPK]), ALU.subtract)\
                    .then_inc(*mark("topk_diff", k, t))
                yield ("choose", t, 7)
                dve.wait_ge(*after("topk_exp", k, t))
                d(V.tensor_reduce(e_sum, bv, AX_X, ALU.add))
                settle()
                d(V.reciprocal(e_sum, e_sum))
                settle()
                V.tensor_tensor(gates[:, at:at + PICKS].rearrange("p (h k) -> p h k", h=PEER_HEADS), bv,
                                e_sum.unsqueeze(2).broadcast_to([P, PEER_HEADS, TOPK]), ALU.mult)\
                    .then_inc(*mark("picked", k, t))
                dve.wait_ge(*after("picked", k, t))
                yield ("exp", t)

            def dense(st):
                k, T, N = st.k, st.T, st.N
                yield "start"
                modulate(st, 0)
                yield "h1"
                if st.lat:
                    dve.wait_ge(*after("par_in", st.layer))
                    pr = lam_in.rearrange("p (a b) -> p a b", a=4)
                    d(V.tensor_tensor_reduce(pr[:, 0, :], pr[:, 0, :], pr[:, 1, :], 1.0, 0.0, ALU.mult, ALU.add, dot2[:, 0:1]))
                    d(V.tensor_tensor(d_sum, d_skip[:, 0:4], d_skip[:, 4:8], ALU.add))
                    V.tensor_tensor_reduce(pr[:, 2, :], pr[:, 2, :], pr[:, 3, :], 1.0, 0.0, ALU.mult, ALU.add, dot2[:, 1:2])\
                        .then_inc(*mark("par_lam", st.layer))
                d(V.memset(xraw[:, :, 0:2], 0.0))
                d(V.memset(xraw[:, :, N + 2:N + 4], 0.0))
                if st.lat:
                    for t in range(T):
                        dve.wait_ge(*taken("q", k, t))
                        dve.wait_ge(*taken("k", k, t))
                        q4 = qk[t].rearrange("p (u x s i) -> p u x s i", u=16, x=2, s=2)
                        r4 = rope_tmp.rearrange("p (u x s i) -> p u x s i", u=16, x=2, s=2)
                        sin = c("sin", 64 * t, 64).rearrange("p (x s i) -> p x s i", x=2, s=2)
                        for s in range(2):
                            d(V.tensor_tensor(r4[:, :, :, s, :], q4[:, :, :, 1 - s, :],
                                              sin[:, :, s, :].unsqueeze(1).broadcast_to([P, 16, 2, 16]), ALU.mult))
                        settle()
                        q3 = qk[t].rearrange("p (u i) -> p u i", u=16)
                        d(V.tensor_tensor(q3, q3, c("cos", 64 * t, 64).unsqueeze(1).broadcast_to([P, 16, 64]), ALU.mult))
                        settle()
                        V.tensor_tensor(qk[t], qk[t], rope_tmp, ALU.add).then_inc(*mark("rope", k, t))
                        dve.wait_ge(*after("rope", k, t))
                    dve.wait_ge(*taken("par", st.layer))
                    dve.wait_ge(*after("par_ready", st.layer))
                    d(V.tensor_scalar(a_log, a_log, -1.0, None, ALU.mult))
                    dve.wait_ge(*after("lam", st.layer))
                    d(V.tensor_tensor(lam, dot2[:, 0:1], dot2[:, 1:2], ALU.subtract))
                    settle()
                    d(V.scalar_tensor_tensor(lam, lam, -1.0, c("lam", st.layer, 1), ALU.mult, ALU.subtract))
                    d(V.tensor_tensor(subln_s, subln, c("lam", DEPTH + st.layer, 1), ALU.mult))
                    settle()
                yield "rope"
                for b in range(CONV_BLOCKS):
                    dve.wait_ge(*taken("xb", k, b))
                settle()
                for j in range(TAPS):
                    for b in range(CONV_BLOCKS):
                        o, src, w = conv[:, b, 0:N], xraw[:, b, j:j + N], conv_w[:, b, j:j + 1]
                        if j == 0:
                            d(V.tensor_scalar(o, src, w, conv_b[:, b:b + 1], ALU.mult, ALU.add))
                        elif j == TAPS - 1 and b == CONV_BLOCKS - 1:
                            V.scalar_tensor_tensor(o, src, w, o, ALU.mult, ALU.add).then_inc(*mark("conv_sum", k))
                        else:
                            d(V.scalar_tensor_tensor(o, src, w, o, ALU.mult, ALU.add))
                    settle()
                yield "conv"
                n = 8 * T
                u, w1, ln = dt_u[:, 0:n], dt_u[:, 16:16 + n], dt_u[:, 32:32 + n]
                dv, tmp = dt[:, 0:n], dt_tmp[:, 0:n]
                dve.wait_ge(*taken("dt", k, T - 1))
                d(V.tensor_tensor(dv.rearrange("p (t h) -> p t h", h=8), dtraw[:, 0:n].rearrange("p (t h) -> p t h", h=8),
                                  dt_bias.unsqueeze(1).broadcast_to([P, T, 8]), ALU.add))
                settle()
                d(V.tensor_scalar(u, dv, -1.0, None, ALU.mult))
                settle()
                V.tensor_tensor(u, u, dv, ALU.max).then_inc(*mark("dt_abs", k))
                dve.wait_ge(*after("dt_exp", k))
                V.tensor_scalar(w1, u, 1.0, None, ALU.add).then_inc(*mark("dt_sum", k))
                dve.wait_ge(*after("dt_ln", k))
                d(V.tensor_scalar(w1, w1, 1.0, None, ALU.subtract))
                settle()
                d(V.tensor_scalar(tmp, w1, 0.0, None, ALU.is_equal))
                settle()
                d(V.tensor_tensor(w1, w1, tmp, ALU.add))
                d(V.tensor_tensor(ln, ln, u, ALU.mult))
                d(V.tensor_tensor(tmp, tmp, u, ALU.mult))
                d(V.tensor_scalar(dv, dv, 0.0, None, ALU.max))
                settle()
                d(V.reciprocal(w1, w1))
                d(V.tensor_tensor(dv, dv, tmp, ALU.add))
                settle()
                d(V.tensor_tensor(ln, ln, w1, ALU.mult))
                settle()
                d(V.tensor_tensor(dv, dv, ln, ALU.add))
                settle()
                V.tensor_tensor(dta[:, 0:n].rearrange("p (t h) -> p t h", h=8), dv.rearrange("p (t h) -> p t h", h=8),
                                a_log.unsqueeze(1).broadcast_to([P, T, 8]), ALU.mult).then_inc(*mark("dta", k))
                dve.wait_ge(*full("cum", k))
                cp = bank("cum", k)[:, 0:24 * T].rearrange("p (t n) -> p t n", t=T)
                cs = cumsum[:, 0:24 * T].rearrange("p (t n) -> p t n", t=T)
                ne = dt_end[:, 0:n].rearrange("p (t n) -> p t n", t=T)
                V.tensor_copy(cs[:, :, 0:16], cp[:, :, 0:16]).then_inc(*take("cum", k))
                dve.wait_ge(*taken("cum", k))
                d(V.tensor_scalar(ne, cs[:, :, 0:8], -1.0, None, ALU.mult))
                V.tensor_tensor(cs[:, :, 16:24], cs[:, :, 8:16], cs[:, :, 0:8], ALU.subtract).then_inc(*mark("nacs", k))
                dve.wait_ge(*after("decays", k))
                d(V.tensor_tensor(dt_tmp[:, 0:n].rearrange("p (t n) -> p t n", t=T), dv.rearrange("p (t n) -> p t n", t=T),
                                  cs[:, :, 16:24], ALU.mult))
                settle()
                yield "dt"
                for s in range(2):
                    t = s if st.lat else 0
                    dve.wait_ge(*taken("xbn", k, t))
                    V.tensor_tensor(xw[:, s * 256:(s + 1) * 256].rearrange("p (h n) -> p h n", h=4),
                                    nat[t][:, 0:256].rearrange("p (h n) -> p h n", h=4),
                                    dt_tmp[:, 8 * t + 4 * s:8 * t + 4 * s + 4].unsqueeze(2).broadcast_to([P, 4, 64]),
                                    ALU.mult).then_inc(*mark("xw", k, s))
                if st.lat:
                    dve.wait_ge(*taken("init", k))
                    for s in range(2):
                        d(V.tensor_tensor(enter1[:, s * 256:(s + 1) * 256].rearrange("p (h n) -> p h n", h=4),
                                          enter0[:, s * 256:(s + 1) * 256].rearrange("p (h n) -> p h n", h=4),
                                          cs[:, s, 8 + 4 * s:12 + 4 * s].unsqueeze(2).broadcast_to([P, 4, 64]), ALU.mult))
                    settle()
                    dve.wait_ge(*full("st", k))
                    V.tensor_tensor(enter1, enter1, bank("st", k)[:, :], ALU.add).then_inc(*take("st", k))
                    dve.wait_ge(*taken("st", k))
                yield "xw"
                for t in range(T):
                    if t:
                        dve.wait_ge(*full("seg", k, t - 1, 1))
                    V.tensor_copy(dta_rep.rearrange("p (h n) -> p h n", h=8),
                                  dta[:, 8 * t:8 * t + 8].unsqueeze(2).broadcast_to([P, 8, P])).then_inc(*mark("rep", k, t))
                    for s in range(2):
                        dve.wait_ge(*taken("seg", k, t, s))
                    dec = decay.rearrange("p (h n) -> p h n", h=8)
                    d(V.tensor_tensor(dec, dec, dt[:, 8 * t:8 * t + 8].unsqueeze(2).broadcast_to([P, 8, P]), ALU.mult))
                    settle()
                    if t:
                        dve.wait_ge(*full("y", k, t - 1))
                    d(V.tensor_tensor(mixed, decay[:, 0:512], decay[:, 512:1024], ALU.add))
                    settle()
                    dve.wait_ge(*full("cb", k, t))
                    m4 = mixed.rearrange("p (g r n) -> p g r n", g=2, r=2)
                    cb = bank("cb", k, t)[:, 0:256].rearrange("p (g n) -> p g n", g=2).unsqueeze(2).broadcast_to([P, 2, 2, P])
                    d(V.tensor_tensor(m4, m4, cb, ALU.mult))
                    settle()
                    V.memset(dot2[:, 2:3], 0.0).then_inc(*take("cb", k, t))
                    V.memset(dot2[:, 3:4], 0.0).then_inc(*mark("M", k, t))
                    y3 = y_nat[t].rearrange("p (h n) -> p h n", h=4)
                    d(V.tensor_tensor(y3, nat[t][:, 0:256].rearrange("p (h n) -> p h n", h=4),
                                      d_sum.unsqueeze(2).broadcast_to([P, 4, 64]), ALU.mult))
                    settle()
                    if st.lat:
                        dve.wait_ge(*full("yo", k, t))
                        V.tensor_tensor(decay[:, 0:512].rearrange("p (h n) -> p h n", h=8),
                                        bank("yo", k, t)[:, :].rearrange("p (h n) -> p h n", h=8),
                                        cs[:, t, 0:8].unsqueeze(2).broadcast_to([P, 8, 64]), ALU.mult)\
                            .then_inc(*take("yo", k, t))
                        dve.wait_ge(*taken("yo", k, t))
                        d(V.tensor_tensor(y_nat[t], y_nat[t], decay[:, 0:256], ALU.add))
                        settle()
                        d(V.tensor_tensor(y_nat[t], y_nat[t], decay[:, 256:512], ALU.add))
                        settle()
                    dve.wait_ge(*full("y", k, t))
                    V.tensor_tensor(y_nat[t], y_nat[t], bank("y", k, t)[:, 0:256], ALU.add).then_inc(*take("y", k, t))
                    dve.wait_ge(*taken("y", k, t))
                    dve.wait_ge(*after("silu_z", k, t))
                    d(V.tensor_tensor(y_nat[t], y_nat[t], pz[t][:, 256:512], ALU.mult))
                    settle()
                    d(V.tensor_tensor_reduce(pz[t][:, 256:512], y_nat[t], y_nat[t], 1.0, 0.0, ALU.mult, ALU.add, ss[:, 2:3]))
                    settle()
                    inverse_rms(rstd[:, 2:3], ss[:, 2:3], 256)
                    V.tensor_scalar(y_nat[t], y_nat[t], rstd[:, 2:3], None, ALU.mult).then_inc(*mark("y_n", k, t))
                    yield ("seg", t)
                yield "y"
                heads = [(t, h) for t in range(T) for h in range(ATT_HEADS)]

                def row_max(i):
                    t, h = heads[i]
                    for m in range(2):
                        dve.wait_ge(*full("s", k, t, h, m))
                        d(V.reduce_max(mx[i % 2][:, m:m + 1], bank("s", k, t, h, m)[:, 0:st.NK], AX_X))
                    settle()
                    V.tensor_scalar(mx[i % 2], mx[i % 2], -ATT_SCALE, None, ALU.mult).then_inc(*mark("mx", k, t, h))

                row_max(0)
                for i, (t, h) in enumerate(heads):
                    if i + 1 < len(heads):
                        row_max(i + 1)
                    for m in range(2):
                        dve.wait_ge(*taken("s", k, t, h, m))
                    sm = sums[i % 2]
                    d(V.reciprocal(sm, sm))
                    settle()
                    d(V.tensor_scalar(sm[:, 1:2], sm[:, 1:2], lam, None, ALU.mult))
                    p0, p1 = (prob[i % 2][m][:, 0:st.NK] for m in range(2))
                    d(V.tensor_scalar(p0, p0, sm[:, 0:1], None, ALU.mult))
                    settle()
                    V.scalar_tensor_tensor(p0, p1, sm[:, 1:2], p0, ALU.mult, ALU.add).then_inc(*mark("aw", k, t, h))
                    if h == ATT_HEADS - 1:
                        dve.wait_ge(*taken("o", k, t, h))
                        o3 = o_nat.rearrange("p (h n) -> p h n", h=4)
                        d(V.tensor_tensor(mixed, o_nat, o_nat, ALU.mult))
                        settle()
                        d(V.tensor_reduce(ss[:, 0:4], mixed.rearrange("p (h n) -> p h n", h=4), AX_X, ALU.add))
                        settle()
                        inverse_rms(rstd[:, 0:4], ss[:, 0:4], P)
                        V.tensor_tensor(o3, o3, rstd[:, 0:4].unsqueeze(2).broadcast_to([P, 4, P]), ALU.mult)\
                            .then_inc(*mark("o_n", k, t))
                    if h % 2 == 1:
                        yield ("att", 4 * t + h)
                dve.wait_ge(*after("mod_g1", k, 2))
                for cc in range(2):
                    for t in range(T):
                        tmp = mixed if (cc * T + t) % 2 == 0 else xw
                        g = mod_g1[:, cc * CHUNK:(cc + 1) * CHUNK]
                        xt = x[st.X + t][:, cc * CHUNK:(cc + 1) * CHUNK]
                        dve.wait_ge(*full("wo", k, t, cc))
                        V.tensor_tensor(tmp, bank("wo", k, t, cc)[:, :], g, ALU.mult).then_inc(*take("wo", k, t, cc))
                        dve.wait_ge(*taken("wo", k, t, cc))
                        if cc:
                            V.tensor_tensor(xt, xt, tmp, ALU.add).then_inc(*mark("x_mid", k, t))
                        else:
                            d(V.tensor_tensor(xt, xt, tmp, ALU.add))
                yield "mid"
                modulate(st, 1)
                yield ("ps", 0)
                for t in range(T):
                    if t:
                        yield ("ps", t)
                    yield from choose(st, t)

            def gather(k, which, t, part):
                st = steps[k]
                n = st.X + t
                base, col = pass_base[k, which if which < 2 else 1, t], n * PICKS
                if which == 0:
                    lo, hi = part
                    with dve.Fori(lo, hi) as turn:
                        for r in range(TURN):
                            slot = r % RING
                            dve.wait_ge(row_landed[slot], turn * (16 * TURN // RING) + (16 * (base // RING + r // RING + 1)))
                            V.tensor_tensor_reduce(rows[slot][:, :], rows[slot][:, :], hn[n][:, :], 1.0, 0.0, ALU.mult,
                                                   ALU.add, dots_now[:, r:r + 1]).then_inc(row_used, 1)
                        dve.wait_ge(row_used, turn * TURN + (RING + base + TURN))
                        V.tensor_copy(dots[:, bass.ds(turn * TURN + col, TURN)], dots_now[:, :])\
                            .then_inc(sems["dots_copied"], 1)
                        dve.wait_ge(sems["dots_copied"], turn + (dots_base[k, t] + 1))
                    if hi == PICKS // TURN:
                        V.memset(dot2[:, 2:3], 0.0).then_inc(*mark("act_done", k, t))
                elif which == 2:
                    dve.wait_ge(*after("gelu", k, t))
                    d(V.tensor_tensor(picks_w[:, col:col + PICKS], dots[:, col:col + PICKS], gates[:, col:col + PICKS], ALU.mult))
                    settle()
                else:
                    lo, hi = part
                    if lo == 0:
                        for a in range(2):
                            d(V.memset(acc[a][:, :], 0.0))
                        settle()
                    with dve.Fori(lo, hi) as turn:
                        for r in range(TURN):
                            slot = r % RING
                            dve.wait_ge(row_used, turn * TURN + (RING + base + r - 1))
                            dve.wait_ge(row_landed[slot], turn * (16 * TURN // RING) + (16 * (base // RING + r // RING + 1)))
                            V.scalar_tensor_tensor(acc[r % 2][:, :], rows[slot][:, :],
                                                   picks_w[:, bass.ds(turn * TURN + (col + r), 1)], acc[r % 2][:, :],
                                                   ALU.mult, ALU.add).then_inc(row_used, 1)
                    if hi == PICKS // TURN:
                        dve.wait_ge(row_used, RING + base + PICKS)
                        d(V.tensor_tensor(acc[0][:, :], acc[0][:, :], acc[1][:, :], ALU.add))
                        settle()
                        dve.wait_ge(*after("mod_g2", k, 5))
                        d(V.tensor_tensor(acc[0][:, :], acc[0][:, :], mod_g2[st.s][:, :], ALU.mult))
                        settle()
                        V.tensor_tensor(x[n][:, :], x[n][:, :], acc[0][:, :], ALU.add).then_inc(*mark("x_new", k, t))
                        dve.wait_ge(*after("x_new", k, t))
                        if st.layer == DEPTH - 1:
                            d(V.tensor_tensor_reduce(acc[0][:, :], x[n][:, :], x[n][:, :], 1.0, 0.0, ALU.mult, ALU.add,
                                                     ss[:, 3:4]))
                            settle()
                            inverse_rms(rstd[:, 3:4], ss[:, 3:4], D)
                            dve.wait_ge(*after("fw_in", k))
                            V.scalar_tensor_tensor(x[n][:, :], x[n][:, :], rstd[:, 3:4], hn[st.X][:, :],
                                                   ALU.mult, ALU.mult).then_inc(*mark("y_ready", k, t))

            dots_base, n = {}, 0
            for st in steps:
                for t in range(st.T):
                    dots_base[st.k, t] = n
                    n += PICKS // TURN
            dve.sem_inc(row_used, RING)
            dve.wait_ge(*after("consts_in"))
            run_beside(steps, modulation, dense, gather, True)

    assert sorted(map(str, took)) == sorted(map(str, numbers)), "each psum job is taken once"
    return numbers, M.reached


def pauses_of(st):
    names = []
    if st.lat and st.k:
        names += [(("mod", j), True, 0.5) for j in range(12)]
    names += [("start", True, 0.0), ("h1", False, 2.0), ("rope", True, 2.0), ("conv", True, 0.5), ("dt", True, 0.5),
              ("xw", True, 0.5)]
    names += [(("seg", t), True, 0.5) for t in range(st.T)]
    names += [("y", True, 0.5)]
    names += [(("att", i), True, 0.5) for i in range(1, st.T * ATT_HEADS, 2)]
    names += [("mid", True, 0.5), (("ps", 0), True, 2.0)]
    for t in range(st.T):
        if t:
            names += [(("ps", t), True, 0.0)]
        names += [(("choose", t, i), False, 0.25) for i in range(8)]
        names += [(("exp", t), True, 0.5)]
    return names


def gather_plan(steps, k):
    st = steps[k - 1]
    turns = PICKS // TURN
    todo = [(0, t, (i, i + 1)) for t in range(st.T) for i in range(turns)]
    todo += [(2, t, None) for t in range(st.T)]
    todo += [(1, t, (i, i + 1)) for t in range(st.T) for i in range(turns)]
    plan, done = {}, 0
    names = pauses_of(steps[k]) if k < len(steps) else []
    whole = sum(w for _, _, w in names)
    so_far = 0.0
    for name, common, weight in names:
        so_far += weight
        here = plan.setdefault(name, [])
        while todo and done < int(len(todo_all(st)) * so_far / whole):
            if todo[0][0] == 2 and not common:
                break
            here.append(todo.pop(0))
            done += 1
    plan[None] = todo
    for name in plan:
        plan[name] = joined(plan[name])
    return plan


def todo_all(st):
    return range(2 * st.T * (PICKS // TURN) + st.T)


def joined(parts):
    out = []
    for kind, t, span in parts:
        if span and out and out[-1][0] == kind and out[-1][1] == t:
            out[-1] = (kind, t, (out[-1][2][0], span[1]))
        else:
            out.append((kind, t, span))
    return out


def run_beside(steps, modulation, dense, gather, everything):
    for k in range(len(steps) + 1):
        plan = gather_plan(steps, k) if k else {}

        def beside(name):
            for kind, t, span in plan.get(name, []):
                gather(k - 1, kind, t, span)

        if k < len(steps):
            names = [n for n, common, _ in pauses_of(steps[k]) if everything or common]
            seen = []
            if steps[k].lat:
                for name in modulation(steps[k].layer):
                    if k:
                        seen.append(name)
                        beside(name)
            for name in dense(steps[k]):
                seen.append(name)
                beside(name)
            assert seen == names, (seen, names)
        beside(None)


INPUTS = ["x_prompt", "x_sample", "cache_attn_k", "cache_attn_v", "state_ssd_fwd", "state_ssd_bwd", "c", "c_ctx",
          "mod_w", "mod_b", "norm1_w", "norm2_w", "w_in", "pool_w", "pool_scale", "ssd_conv_w", "ssd_conv_b",
          "ssd_A_log", "ssd_dt_bias", "ssd_D", "ssd_norm_w", "attn_lambda", "attn_subln_w", "w_out", "peer_wq",
          "peer_keys", "peer_u", "peer_v", "final_norm_w"]
OUTPUTS = {"y_prompt": (1, 128, 1024), "y_sample": (1, 256, 1024), "new_k": (1, DEPTH, 128, 4, 128),
           "new_v": (1, DEPTH, 128, 4, 128), "new_f": (1, DEPTH, 4, 64, 128), "new_b": (1, DEPTH, 4, 64, 128)}


def declare(nc, arrays):
    io = {name: nc.dram_tensor(name + "_in", a.shape, F32, kind="ExternalInput").ap() for name, a in arrays.items()}
    for name, shape in OUTPUTS.items():
        io[name] = nc.dram_tensor(name + "_out", shape, F32, kind="ExternalOutput").ap()
    io["mod_scratch"] = nc.dram_tensor("mod_scratch", (DEPTH, 6, 2, D), F32, kind="Internal").ap()
    io["state_fwd"], io["state_bwd"] = io["state_ssd_fwd"], io["state_ssd_bwd"]
    for name in ("peer_u", "peer_v"):
        io[name] = io[name].rearrange("l e d -> (l e) d")
    return io


def kernel(**inputs):
    import concourse.bacc as bacc
    from concourse.bass_utils import run_bass_kernel_spmd

    where, const, band_lat, band_ctx = shape_constants()
    arrays = {name: np.ascontiguousarray(inputs[name]) for name in INPUTS}
    arrays |= {"const": const, "band_lat": band_lat, "band_ctx": band_ctx}
    known = None
    for _ in range(2):
        nc = bacc.Bacc("TRN2", target_bir_lowering=False, num_devices=1)
        known = build_pass(nc, declare(nc, arrays), where, known)
    r = run_bass_kernel_spmd(nc, [{name + "_in": a for name, a in arrays.items()}], core_ids=[0]).results[0]
    return tuple(r[name + "_out"] for name in OUTPUTS)
```

```python
from contextlib import ExitStack

import numpy as np

import concourse.bass as bass
from concourse import mybir

ALU = mybir.AluOpType
ACT = mybir.ActivationFunctionType
F32 = mybir.dt.float32
U32 = mybir.dt.uint32
AX_X = mybir.AxisListType.X

P = 128
D = 1024
DB = D // P
DEPTH = 2
EPS = 1e-6
POOL_WINDOWS = (2, 4, 8, 16)
GRID_W = 64
SSD_HEADS = 4
CONV_BLOCKS = 6
TAPS = 5
ATT_HEADS = 4
ATT_SCALE = 64 ** -0.5
PEER_HEADS = 8
TOPK = 16
EXPERTS = 128 * 128
PICKS = PEER_HEADS * TOPK
CHUNK = 512
BANKS = 8
RING = 8
TURN = 16
PART = 8
CELLS = ((0, 1, 16), (1, 1, 8), (2, 2, 5), (4, 4, 3), (8, 8, 1))
PACKED = sum(rows * columns for _, rows, columns in CELLS)
NEG = -1e30
LOWEST = -3.0e38
STEPS = 2 * DEPTH
W_SLOTS = 2

MOD_ORDER = (2, 3, 0, 1, 4, 5, 8, 9, 6, 7, 10, 11)
MOD_SCALES = (2, 3, 8, 9)
MOD_AT = {"summed": (4,), "states": (5,), "scanned": (8,), ("head", 0): (9,), ("head", 1): (6,), ("head", 2): (7,),
          "late": (10, 11)}

W_IN = {"pz": (0, 512), "xb0": (512, 512), "xb1": (1024, 264), "q": (1288, 512), "k": (1800, 512), "v": (2312, 512)}


def shape_constants():
    j, i = np.arange(P)[:, None], np.arange(P)[None, :]
    parts = {
        "ident": (j == i).astype(np.float32),
        "tri": np.concatenate([(j <= i), (j >= i)], 1).astype(np.float32),
        "mask": np.concatenate([np.where(j <= i, 0.0, NEG), np.where(j >= i, 0.0, NEG)], 1),
        "ones": np.ones((P, P)),
        "iota": np.tile(np.arange(TOPK, dtype=np.float32), (P, 1)),
    }
    n = np.arange(2 * P)
    inv = 1.0 / (np.float32(10000.0) ** (np.arange(0, 32, 2, dtype=np.float32) / np.float32(32)))
    row = (n // GRID_W).astype(np.float32)[:, None] * inv.astype(np.float32)
    col = (n % GRID_W).astype(np.float32)[:, None] * inv.astype(np.float32)
    cos = np.concatenate([np.cos(row), np.cos(row), np.cos(col), np.cos(col)], 1)
    sin = np.concatenate([-np.sin(row), np.sin(row), -np.sin(col), np.sin(col)], 1)
    parts["cos"] = cos.reshape(2, P, 64).transpose(1, 0, 2).reshape(P, 128)
    parts["sin"] = sin.reshape(2, P, 64).transpose(1, 0, 2).reshape(P, 128)
    lam_init = [0.8 - 0.6 * float(np.exp(-0.3 * layer)) for layer in range(DEPTH)]
    parts["lam"] = np.tile(np.array([lam_init + [1.0 - x for x in lam_init]]), (P, 1))
    at, where = 0, {}
    for name, a in parts.items():
        where[name] = (at, a.shape[1])
        at += a.shape[1]
    bands = []
    for length in (2 * P, P):
        t = np.arange(length)
        for w in POOL_WINDOWS:
            lo, hi = np.clip(t - w // 2, 0, length), np.clip(t + w // 2, 0, length)
            b = ((t[:, None] >= lo) & (t[:, None] < hi)) / (hi - lo)[None, :] - np.eye(length)
            bands.append(b.reshape(length // P, P, length).transpose(1, 0, 2).reshape(P, -1))
    lat = np.concatenate(bands[:4], 1).astype(np.float32)
    ctx = np.concatenate(bands[4:], 1).astype(np.float32)
    return where, np.concatenate(list(parts.values()), 1).astype(np.float32), lat, ctx


class Marks:

    def __init__(self, sems, known):
        self.sems, self.known, self.reached, self.total = sems, known, {}, {}

    def mark(self, name, *key, n=1):
        self.total[name] = self.total.get(name, 0) + n
        self.reached[name, *key] = self.total[name]
        return self.sems[name], n

    def after(self, name, *key):
        if not self.known:
            return self.sems[name], 1
        return self.sems[name], self.known[name, *key]


EVENTS = """consts_in x_in cond_in cond_ready par_in par_ready bias_in nw_in row_stored
mod_a mod_b mod_g1 mod_g2 cache_in init_in band_in keys_in newk newv states_out fw_in y_out
ss h1 rope conv_sum conv dt_abs dt_exp dt_sum dt_ln dta nacs decays rep E M xw enter yo_done silu_z y_n
par_lam lam mx aw o_n h2 x_mid topk_diff topk_exp picked picks_copied act_done gelu weights x_new y_ready
pool_step act_step v_step sums o_done dots_copied""".split()


def build_pass(nc, io, where, known):
    jobs, events = known or ({}, {})
    stack = ExitStack()
    with stack:
        def sb(name, cols, dt=F32, rows=P):
            return stack.enter_context(nc.sbuf_tensor(name, [rows, cols], dt))

        sems = {n: stack.enter_context(nc.semaphore(n)) for n in EVENTS}
        for n in range(BANKS):
            sems["psum_full", n] = stack.enter_context(nc.semaphore(f"psum_full{n}"))
            sems["psum_taken", n] = stack.enter_context(nc.semaphore(f"psum_taken{n}"))
        w_landed = [stack.enter_context(nc.semaphore(f"w_landed{n}")) for n in range(W_SLOTS)]
        row_landed = [stack.enter_context(nc.semaphore(f"row_landed{n}")) for n in range(RING)]
        row_used = stack.enter_context(nc.semaphore("row_used"))
        row_go = stack.enter_context(nc.semaphore("row_go"))
        M = Marks(sems, events)
        mark, after = M.mark, M.after
        numbers = {}
        took = []

        x = [sb(f"x{t}", D) for t in range(3)]
        hn = [sb(f"hn{t}", D) for t in range(3)]
        mod_a, mod_b, mod_g1 = sb("mod_a", D), sb("mod_b", D), sb("mod_g1", D)
        mod_g2 = [sb(f"mod_g2{s}", D) for s in range(2)]
        wring = [sb(f"wring{n}", DB * CHUNK) for n in range(W_SLOTS)]
        rows = [sb(f"rows{n}", D) for n in range(RING)]
        acc = [sb(f"acc{n}", D) for n in range(2)]
        work = sb("work", 18220)
        mod_row, mod_bias, mod_nw = sb("mod_row", CHUNK), sb("mod_bias", CHUNK), sb("mod_nw", CHUNK)
        n_const = sum(n for _, n in where.values())
        const = sb("const", n_const)
        par = sb("par", 520)
        small = sb("small", 220)
        idx = sb("idx", 3 * PICKS, U32)
        idx_now = sb("idx_now", TURN, U32)
        gates = sb("gates", 3 * PICKS)
        dots = sb("dots", 3 * PICKS)
        dots_now = sb("dots_now", PART)
        picks_w = sb("picks_w", 3 * PICKS)
        psum = [stack.enter_context(nc.psum_tensor(f"psum{n}", [P, CHUNK], F32)) for n in range(BANKS)]

        def c(name, a=0, n=None):
            at, size = where[name]
            return const[:, at + a:at + (size if n is None else a + n)]

        ident, ones = c("ident"), c("ones")
        tri = [c("tri", 0, P), c("tri", P, P)]
        mask = [c("mask", 0, P), c("mask", P, P)]

        def region(at, n):
            return work[:, at:at + n]

        qk = [region(t * 1024, 1024) for t in range(2)]
        catT = region(0, 2048).rearrange("p (b n) -> p b n", b=8)
        v_nat = [region(2048 + t * 512, 512) for t in range(2)]
        pz = [region(3072 + t * 512, 512) for t in range(2)]
        xraw = region(4096, 1560).rearrange("p (b n) -> p b n", b=6)
        decay = region(4096, 1024)
        conv = region(5656, 1536).rearrange("p (b n) -> p b n", b=6)
        nat = [region(7192 + t * 512, 512) for t in range(2)]
        qT = region(8216, 1024).rearrange("p (h n) -> p h n", h=4)
        kT = region(9240, 1536).rearrange("p (h n) -> p h n", h=4)
        hT = [region(10776, 2048).rearrange("p (b n) -> p b n", b=8),
              region(2048, 2048).rearrange("p (b n) -> p b n", b=8)]
        band = region(10776, 2048)
        prob = [[region(10776 + (2 * a + m) * 384, 384) for m in range(2)] for a in range(2)]
        wT = [region(12312 + a * 384, 384) for a in range(2)]
        k_cached, v_cached = region(13080, 512), region(13592, 512)
        rope_tmp = region(14104, 1024)
        mixed, xw, init_nat = region(14104, 512), region(14616, 512), region(15128, 512)
        enter0, enter1 = region(15640, 512), region(16152, 512)
        y_nat = [region(16664 + t * 256, 256) for t in range(2)]
        o_nat = region(17176, 512)
        pooledT = region(17688, 512).rearrange("p (b n) -> p b n", b=2)
        dta_rep = region(17176, 1024)
        pqT = region(4096, 4096).rearrange("p (b n) -> p b n", b=16)
        keys_nat, keysT = region(8216, 2048), region(10776, 2048)
        scores = region(12824, 2048)
        cand = region(14872, PEER_HEADS * PACKED)
        packed_p, place, passed = (region(15360 + i * PICKS, PICKS) for i in range(3))
        hot = [region(0, 2048), region(2048, 2048)]
        top_v = region(16920, 256)
        top_i = region(17176, 256).bitcast(U32)
        top_f = region(17432, 256)
        best_v = region(17688, 128)
        best_p = region(17816, 128).bitcast(U32)
        half_p = region(17944, 128).bitcast(U32)
        half_f = [region(18072, 128), small[:, 92:220]]
        dtraw = small[:, 0:16]
        ss = small[:, 16:20]
        rstd = small[:, 20:24]
        mx = [small[:, 24 + 2 * a:26 + 2 * a] for a in range(2)]
        sums = [small[:, 28 + 2 * a:30 + 2 * a] for a in range(2)]
        e_sum = small[:, 32:40]
        dot2 = small[:, 40:44]
        cumsum = small[:, 44:92]
        conv_w = par[:, 0:30].rearrange("p (b n) -> p b n", b=6)
        columns = par[:, 30:41]
        conv_b, y_w, pool_s, subln = par[:, 30:36], par[:, 36:38], par[:, 38:40], par[:, 40:41]
        dt_bias, a_log, d_skip = par[:, 42:50], par[:, 50:58], par[:, 58:66]
        d_sum, lam = par[:, 66:70], par[:, 70:71]
        subln_s = par[:, 71:72]
        pool_w = par[:, 72:200].rearrange("p (b n) -> p b n", b=2)
        lam_in = par[:, 200:456]
        dt = par[:, 456:472]
        dta = par[:, 472:488]
        dt_end = par[:, 488:504]
        dt_tmp = par[:, 504:520]
        cond = sb("cond", 16)
        cond3 = cond[:, :].rearrange("p (s b) -> p b s", s=2)
        par_rows = sb("par_rows", P)
        dt_u = sb("dt_u", 48)
        root, root_bits = sb("root", 8), sb("root_bits", 4, U32)

        def job(pe, *key):
            n = len(numbers)
            numbers[key] = n
            if n >= BANKS:
                pe.wait_ge(sems["psum_taken", n % BANKS], n // BANKS)
            return psum[n % BANKS]

        def number(key):
            return jobs.get(key, 0)

        def bank(*key):
            return psum[number(key) % BANKS]

        def made(*key):
            n = numbers.get(key, number(key))
            return sems["psum_full", n % BANKS], 1

        def full(*key):
            return sems["psum_full", number(key) % BANKS], number(key) // BANKS + 1

        def take(*key):
            took.append(key)
            return sems["psum_taken", number(key) % BANKS], 1

        def taken(*key):
            return sems["psum_taken", number(key) % BANKS], number(key) // BANKS + 1

        class Step:
            def __init__(self, k):
                self.k, self.layer, self.s = k, k // 2, 1 - k % 2
                self.first = k % 2 == 0
                self.lat = self.s == 0
                self.T = 2 - self.s
                self.X = 2 * self.s
                self.N = P * self.T
                self.NK = self.N + (P if self.lat else 0)

        steps = [Step(k) for k in range(STEPS)]

        chunks = []
        for st in steps:
            if st.first:
                chunks += [(("mod", st.layer, j), ("mod", st.layer, j)) for j in MOD_ORDER[:4]]
            k, last = st.k, st.T - 1
            chunks += [(("q", k), ("q", k, last)), (("k", k), ("k", k, last)), (("v", k), ("v", k, last)),
                       (("xb1", k), ("xb", k, 5)), (("xb0", k), ("xb", k, 3)), (("pz", k), ("pz", k, last))]
            if st.first:
                chunks += [(("mod", st.layer, j), ("mod", st.layer, j)) for j in MOD_ORDER[4:10]]
            chunks += [(("wo", k, cc), ("wo", k, last, cc)) for cc in range(2)]
            chunks += [(("wq", k, cc), ("pq", k, 4 * cc + 3)) for cc in range(4)]
            if st.first:
                chunks += [(("mod", st.layer, j), ("mod", st.layer, j)) for j in MOD_ORDER[10:]]
        chunk_no = {key: n for n, (key, _) in enumerate(chunks)}

        def chunk(*key):
            return wring[chunk_no[key] % W_SLOTS][:, :].rearrange("p (b n) -> p b n", b=DB)

        def chunk_landed(*key):
            n = chunk_no[key]
            return w_landed[n % W_SLOTS], 16 * (n // W_SLOTS + 1)

        passes = [(st.k, v, t) for st in steps for v in range(2) for t in range(st.T)]
        pass_base = {key: n * PICKS for n, key in enumerate(passes)}

        block = stack.enter_context(nc.Block())

        @block.sync
        def _(sp):
            def load(dst, src, name, *key):
                sp.dma_start(dst, src).then_inc(*mark(name, *key, n=16))

            def load_chunk(*key):
                n = chunk_no[key]
                if n >= W_SLOTS:
                    sp.wait_ge(*full(*chunks[n - W_SLOTS][1]))
                kind = key[0]
                if kind == "mod":
                    src, width = io["mod_w"][key[1], :, key[2] * CHUNK:(key[2] + 1) * CHUNK], CHUNK
                elif kind == "wo":
                    src, width = io["w_out"][key[1] // 2, :, key[2] * CHUNK:(key[2] + 1) * CHUNK], CHUNK
                elif kind == "wq":
                    src, width = io["peer_wq"][key[1] // 2, :, key[2] * CHUNK:(key[2] + 1) * CHUNK], CHUNK
                else:
                    at, width = W_IN[kind]
                    src = io["w_in"][key[1] // 2, :, at:at + width]
                sp.dma_start(chunk(*key)[:, :, 0:width], src.rearrange("(b p) n -> p b n", p=P))\
                  .then_inc(w_landed[n % W_SLOTS], 16)

            def load_params(layer):
                if layer:
                    last = steps[2 * layer - 1]
                    sp.wait_ge(*taken("pm", last.k, 1))
                    sp.wait_ge(*taken("oT", last.k, last.T - 1))

                def row(dst, src, n):
                    load(dst, src.rearrange("(a n) -> a n", a=1).broadcast_to([P, n]), "par_in", layer)
                load(conv_w, io["ssd_conv_w"][layer].rearrange("(b p) n -> p b n", p=P), "par_in", layer)
                if layer == 0:
                    sp.wait_ge(*full("cond"))
                at = 0
                for name, n in (("ssd_conv_b", 6), ("ssd_norm_w", 2), ("pool_scale", 2), ("attn_subln_w", 1)):
                    load(par_rows[at:at + n, :], io[name][layer].rearrange("(b p) -> b p", p=P), "par_in", layer)
                    at += n
                row(dt_bias, io["ssd_dt_bias"][layer].rearrange("a b -> (a b)"), 8)
                row(a_log, io["ssd_A_log"][layer].rearrange("a b -> (a b)"), 8)
                row(d_skip, io["ssd_D"][layer].rearrange("a b -> (a b)"), 8)
                load(pool_w, io["pool_w"][layer].rearrange("(b g) c d -> (g c) b d", g=2), "par_in", layer)
                row(lam_in, io["attn_lambda"][layer].rearrange("a b -> (a b)"), 256)

            def store_row(layer, j):
                sp.wait_ge(*taken("mod", layer, j))
                sp.dma_start(io["mod_scratch"][layer, j // 2, :, (j % 2) * CHUNK:(j % 2 + 1) * CHUNK],
                             mod_row[0:2, :]).then_inc(*mark("row_stored", layer, j, n=16))

            def modulation(layer, order):
                for j in order:
                    n = MOD_ORDER.index(j)
                    before = (layer, MOD_ORDER[n - 1]) if n else (layer - 1, MOD_ORDER[-1])
                    load_chunk("mod", layer, j)
                    if n or layer:
                        sp.wait_ge(*full("mod", *before))
                    load(mod_bias[0:1, :], io["mod_b"][layer:layer + 1, j * CHUNK:(j + 1) * CHUNK], "bias_in", layer, j)
                    if j in MOD_SCALES:
                        w = io["norm1_w"] if j < 6 else io["norm2_w"]
                        i = MOD_SCALES.index(j)
                        if i or layer:
                            sp.wait_ge(*taken("mod", *((layer, MOD_SCALES[i - 1]) if i else (layer - 1, MOD_SCALES[-1]))))
                        load(mod_nw[0:2, :], w[layer:layer + 1, (j % 2) * CHUNK:(j % 2 + 1) * CHUNK]
                             .broadcast_to([2, CHUNK]), "nw_in", layer, j)
                    if j != order[0]:
                        store_row(*before)

            def mod_vector(dst, st, vec, name):
                sp.wait_ge(*after("row_stored", st.layer, 2 * vec + 1))
                load(dst[:, :], io["mod_scratch"][st.layer, vec, st.s:st.s + 1, :].broadcast_to([P, D]), name, st.k, vec)

            def norm1_vectors(st):
                if st.k:
                    sp.wait_ge(*after("h2", st.k - 1, steps[st.k - 1].T - 1))
                mod_vector(mod_a, st, 1, "mod_a")
                mod_vector(mod_b, st, 0, "mod_b")

            def other_vectors(st):
                if st.k:
                    sp.wait_ge(*after("x_mid", st.k - 1, steps[st.k - 1].T - 1))
                mod_vector(mod_g1, st, 2, "mod_g1")
                sp.wait_ge(*after("h1", st.k, st.T - 1))
                mod_vector(mod_a, st, 4, "mod_a")
                mod_vector(mod_b, st, 3, "mod_b")

            def gate2(st):
                if st.k >= 2:
                    sp.wait_ge(*after("x_new", st.k - 2, st.T - 1))
                mod_vector(mod_g2[st.s], st, 5, "mod_g2")

            load(const[:, :], io["const"], "consts_in")
            for s, src in enumerate((io["c"][0], io["c_ctx"])):
                load(par_rows[8 * s:8 * s + 8, :], src.rearrange("(b p) -> b p", p=P), "cond_in")
            for st in steps:
                k, layer = st.k, st.layer
                if st.first:
                    modulation(layer, MOD_ORDER[:4])
                    if k == 0:
                        load(x[2][:, :], io["x_prompt"][0], "x_in", 2)
                        for t in range(2):
                            load(x[t][:, :], io["x_sample"][0, t * P:(t + 1) * P, :], "x_in", t)
                    load_chunk("q", k)
                    store_row(layer, MOD_ORDER[3])
                    norm1_vectors(st)
                    load_params(layer)
                else:
                    load_chunk("q", k)
                load_chunk("k", k)
                if st.lat:
                    sp.wait_ge(*after("h1", k, st.T - 1))
                    load(k_cached, io["cache_attn_k"][0, layer].rearrange("n h d -> n (h d)"), "cache_in", layer)
                    load(v_cached, io["cache_attn_v"][0, layer].rearrange("n h d -> n (h d)"), "cache_in", layer)
                load_chunk("v", k)
                load_chunk("xb1", k)
                if not st.lat:
                    sp.wait_ge(*taken("k", k, 0))
                    sp.dma_start(io["new_k"][0, layer].rearrange("n h d -> n (h d)"), qk[0][:, 512:1024])\
                      .then_inc(*mark("newk", layer, n=16))
                load_chunk("xb0", k)
                load_chunk("pz", k)
                if not st.lat:
                    sp.wait_ge(*taken("v", k, 0))
                    sp.dma_start(io["new_v"][0, layer].rearrange("n h d -> n (h d)"), v_nat[0])\
                      .then_inc(*mark("newv", layer, n=16))
                sp.wait_ge(*full("pz", k, st.T - 1))
                load(band[:, 0:4 * st.T * st.N], io["band_lat" if st.lat else "band_ctx"], "band_in", k)
                if st.first:
                    modulation(layer, MOD_ORDER[4:10])
                if st.lat:
                    sp.wait_ge(*after("rope", k, 1))
                    for d, name in enumerate(("state_fwd", "state_bwd")):
                        load(init_nat[:, d * 256:(d + 1) * 256].rearrange("p (g n) -> p g n", g=2),
                             io[name][0, layer].rearrange("(g h) p n -> (h p) g n", g=2), "init_in", layer)
                load_chunk("wo", k, 0)
                if st.first:
                    store_row(layer, MOD_ORDER[9])
                other_vectors(st)
                load_chunk("wo", k, 1)
                if not st.lat:
                    sp.wait_ge(*taken("st", k))
                    for d, name in enumerate(("new_f", "new_b")):
                        sp.dma_start(io[name][0, layer].rearrange("(g h) p n -> (h p) g n", g=2),
                                     enter0[:, d * 256:(d + 1) * 256].rearrange("p (g n) -> p g n", g=2))\
                          .then_inc(*mark("states_out", layer, n=16))
                sp.wait_ge(*full("s", k, st.T - 1, ATT_HEADS - 1, 1))
                load(keys_nat.rearrange("p (b n) -> p b n", b=16),
                     io["peer_keys"][layer].rearrange("m h n d -> n (m h) d"), "keys_in", k)
                for cc in range(4):
                    load_chunk("wq", k, cc)
                    if cc == 2 and st.first:
                        norm1_vectors(steps[k + 1])
                if st.first:
                    modulation(layer, MOD_ORDER[10:])
                    store_row(layer, MOD_ORDER[11])
                gate2(st)
            for st in steps[-2:]:
                for t in range(st.T):
                    sp.wait_ge(*after("act_done", st.k, t))
                load(hn[st.X][:, :], io["final_norm_w"].rearrange("(a n) -> a n", a=1).broadcast_to([P, D]), "fw_in", st.k)
                for t in range(st.T):
                    sp.wait_ge(*after("y_ready", st.k, t))
                    dst = io["y_sample"][0, t * P:(t + 1) * P, :] if st.lat else io["y_prompt"][0]
                    sp.dma_start(dst, x[st.X + t][:, :]).then_inc(*mark("y_out", st.k, t, n=16))
            sp.wait_ge(*after("y_out", STEPS - 1, steps[-1].T - 1))
            sp.wait_ge(*after("newk", DEPTH - 1))
            sp.wait_ge(*after("newv", DEPTH - 1))
            sp.wait_ge(*after("states_out", DEPTH - 1))

        @block.gpsimd
        def _(pool):
            tables = [io["peer_u"], io["peer_v"]]
            half = TURN // 2
            for n, (k, which, t) in enumerate(passes):
                if which == 0:
                    pool.wait_ge(*after("picked", k, t))
                base, col = pass_base[k, which, t], (steps[k].X + t) * PICKS
                with pool.Fori(0, PICKS // TURN) as turn:
                    for part in range(2):
                        q = turn * TURN + (base + part * half)
                        pool.wait_ge(row_used, q + 1)
                        pool.sem_inc(row_go, 1)
                        nc.gpsimd.tensor_copy(idx_now[:, part * half:(part + 1) * half],
                                              idx[:, bass.ds(turn * TURN + (col + part * half), half)])\
                            .then_inc(sems["picks_copied"], 1)
                        pool.wait_ge(sems["picks_copied"], turn * 2 + (n * 2 * (PICKS // TURN) + part + 1))
                        for r in range(half):
                            if r % 2 == 0:
                                pool.wait_ge(row_used, q + (r + 2))
                                pool.sem_inc(row_go, 1)
                            nc.gpsimd.indirect_dma_start(
                                rows[r][:, :], None, tables[which],
                                bass.IndirectOffsetOnAxis(ap=idx_now[:, part * half + r:part * half + r + 1], axis=0))\
                                .then_inc(row_landed[r], 16)

        @block.tensor
        def _(pe):
            mm, tr = nc.tensor.matmul, nc.tensor.transpose

            def modulation(layer, order):
                if layer == 0 and order[0] == MOD_ORDER[0]:
                    pe.wait_ge(*after("consts_in"))
                    pe.wait_ge(*after("cond_in"))
                    p = job(pe, "cond")
                    tr(p[:, 0:16], par_rows[0:16, :], ident[0:16, 0:16]).then_inc(*made("cond"))
                    pe.wait_ge(*taken("cond"))
                for j in order:
                    p = job(pe, "mod", layer, j)
                    pe.wait_ge(*chunk_landed("mod", layer, j))
                    w = chunk("mod", layer, j)
                    for b in range(DB):
                        mm(p[0:2, :], cond3[:, b, :], w[:, b, :], start=(b == 0), stop=False)
                    pe.wait_ge(*after("bias_in", layer, j))
                    mm(p[0:2, :], ones[0:1, 0:2], mod_bias[0:1, :], start=False, stop=True)\
                        .then_inc(*made("mod", layer, j))

            def modulate_at(st, point):
                if st.first:
                    modulation(st.layer, MOD_AT[point])

            def turn_h(st, which):
                name = ("hT1", "hT2")[which]
                for t in range(st.T):
                    pe.wait_ge(*after(("h1", "h2")[which], st.k, t))
                    for half in range(2):
                        p = job(pe, name, st.k, t, half)
                        for i in range(4):
                            b = 4 * half + i
                            ins = tr(p[:, i * P:(i + 1) * P], hn[st.X + t][:, b * P:(b + 1) * P], ident)
                        ins.then_inc(*made(name, st.k, t, half))

            def project(st, name, n, slot=0, key=None):
                k = st.k
                key = key or (name, k)
                pe.wait_ge(*chunk_landed(*key))
                w = chunk(*key)
                for t in range(st.T):
                    jk = (name, k, t)
                    p = job(pe, *jk)
                    for b in range(DB):
                        ins = mm(p[:, 0:n], hT[0][:, b, t * P:(t + 1) * P], w[:, b, slot:slot + n],
                                 start=(b == 0), stop=(b == DB - 1))
                    ins.then_inc(*made(*jk))

            def conv_project(st, blocks, key):
                pe.wait_ge(*chunk_landed(*key))
                w = chunk(*key)
                for i, bb in enumerate(blocks):
                    p = job(pe, "xb", st.k, bb)
                    for b in range(DB):
                        ins = mm(p[:, 0:st.N], w[:, b, i * P:(i + 1) * P], hT[0][:, b, 0:st.N],
                                 start=(b == 0), stop=(b == DB - 1))
                    ins.then_inc(*made("xb", st.k, bb))

            def dense(st):
                k, T, N = st.k, st.T, st.N
                if st.first:
                    p = job(pe, "par", st.layer)
                    pe.wait_ge(*after("par_in", st.layer))
                    tr(p[:, 0:11], par_rows[0:11, :], ident[0:11, 0:11]).then_inc(*made("par", st.layer))
                turn_h(st, 0)
                pe.wait_ge(*taken("hT1", k, T - 1, 1))
                project(st, "q", CHUNK)
                project(st, "k", CHUNK)
                project(st, "v", CHUNK)
                project(st, "dt", 8, slot=256, key=("xb1", k))
                conv_project(st, range(4, 6), ("xb1", k))
                conv_project(st, range(4), ("xb0", k))
                project(st, "pz", CHUNK)
                p = job(pe, "cum", k)
                pe.wait_ge(*after("dta", k))
                for t in range(T):
                    o = 24 * t
                    mm(p[:, o:o + 4], tri[0], dta[:, 8 * t:8 * t + 4], start=True, stop=True)
                    mm(p[:, o + 4:o + 8], tri[1], dta[:, 8 * t + 4:8 * t + 8], start=True, stop=True)
                    ins = mm(p[:, o + 8:o + 16], ones, dta[:, 8 * t:8 * t + 8], start=True, stop=True)
                ins.then_inc(*made("cum", k))
                for t in range(T):
                    if st.lat:
                        pe.wait_ge(*after("rope", k, t))
                    else:
                        pe.wait_ge(*taken("k", k, t))
                    for side in range(2):
                        p = job(pe, "qkT", k, t, side)
                        for h in range(4):
                            at = side * 512 + h * P
                            ins = tr(p[:, h * P:(h + 1) * P], qk[t][:, at:at + P], ident)
                        ins.then_inc(*made("qkT", k, t, side))
                if st.lat:
                    p = job(pe, "kc", k)
                    pe.wait_ge(*after("cache_in", st.layer))
                    for h in range(4):
                        ins = tr(p[:, h * P:(h + 1) * P], k_cached[:, h * P:(h + 1) * P], ident)
                    ins.then_inc(*made("kc", k))
                pe.wait_ge(*after("band_in", k))
                for pair in range(2):
                    p = job(pe, "pl", k, pair)
                    for r in range(2):
                        g = 2 * pair + r
                        for ti in range(T):
                            ins = mm(p[64 * r:64 * r + 64, 0:N], pz[ti][:, g * 64:(g + 1) * 64],
                                     band[:, (g * T + ti) * N:(g * T + ti + 1) * N], start=(ti == 0), stop=(ti == T - 1))
                    ins.then_inc(*made("pl", k, pair))
                for pair in range(2):
                    p = job(pe, "pm", k, pair)
                    pe.wait_ge(*taken("pl", k, pair))
                    for r in range(2):
                        ins = mm(p[64 * r:64 * r + 64, 0:N], pool_w[64 * r:64 * r + 64, pair, :],
                                 pooledT[64 * r:64 * r + 64, pair, 0:N], start=True, stop=True)
                    ins.then_inc(*made("pm", k, pair))
                modulate_at(st, "summed")
                pe.wait_ge(*after("conv", k))
                for t in range(T):
                    p = job(pe, "xbn", k, t)
                    for b in range(4):
                        ins = tr(p[:, b * P:(b + 1) * P], conv[:, b, t * P:(t + 1) * P], ident)
                    ins.then_inc(*made("xbn", k, t))
                if st.lat:
                    p = job(pe, "init", k)
                    pe.wait_ge(*after("init_in", st.layer))
                    for b in range(4):
                        ins = tr(p[:, b * P:(b + 1) * P], init_nat[:, b * P:(b + 1) * P], ident)
                    ins.then_inc(*made("init", k))
                p = job(pe, "st", k)
                for d in range(2):
                    t = d if st.lat else 0
                    pe.wait_ge(*after("xw", k, d))
                    for g in range(2):
                        o = d * 256 + g * P
                        b_nat = nat[t][:, 256 + g * P:256 + (g + 1) * P]
                        x_w = xw[:, o:o + P]
                        ins = mm(p[:, o:o + P], *((b_nat, x_w) if st.lat else (x_w, b_nat)), start=True, stop=True)
                ins.then_inc(*made("st", k))
                modulate_at(st, "states")
                for t in range(T):
                    p = job(pe, "cb", k, t)
                    for g in range(2):
                        ins = mm(p[:, g * P:(g + 1) * P], conv[:, 2 + g, t * P:(t + 1) * P],
                                 conv[:, 4 + g, t * P:(t + 1) * P], start=True, stop=True)
                    ins.then_inc(*made("cb", k, t))
                    pe.wait_ge(*after("rep", k, t))
                    for d in range(2):
                        p = job(pe, "seg", k, t, d)
                        mm(p[:, :].rearrange("p (h n) -> p h n", h=4), ident,
                           mask[d].unsqueeze(1).broadcast_to([P, 4, P]), start=True, stop=False)
                        for h in range(4):
                            ins = mm(p[:, h * P:(h + 1) * P], dta_rep[:, (4 * d + h) * P:(4 * d + h + 1) * P], tri[d],
                                     start=False, stop=(h == 3))
                        ins.then_inc(*made("seg", k, t, d))
                    if st.lat:
                        p = job(pe, "yo", k, t)
                        pe.wait_ge(*taken("init", k))
                        pe.wait_ge(*taken("st", k))
                        for d in range(2):
                            state = enter0 if d == t else enter1
                            for g in range(2):
                                o = d * 256 + g * P
                                ins = mm(p[:, o:o + P], conv[:, 4 + g, t * P:(t + 1) * P], state[:, o:o + P],
                                         start=True, stop=True)
                        ins.then_inc(*made("yo", k, t))
                    p = job(pe, "y", k, t)
                    pe.wait_ge(*after("M", k, t))
                    for h in range(4):
                        ins = mm(p[:, h * 64:(h + 1) * 64], mixed[:, h * P:(h + 1) * P], nat[t][:, h * 64:(h + 1) * 64],
                                 start=True, stop=True)
                    ins.then_inc(*made("y", k, t))
                modulate_at(st, "scanned")
                for t in range(T):
                    p = job(pe, "yT", k, t)
                    pe.wait_ge(*after("y_n", k, t))
                    for b in range(2):
                        ins = tr(p[:, b * P:(b + 1) * P], y_nat[t][:, b * P:(b + 1) * P], ident)
                    ins.then_inc(*made("yT", k, t))
                heads = [(t, h) for t in range(T) for h in range(ATT_HEADS)]

                def scores_of(t, h):
                    for m in range(2):
                        p = job(pe, "s", k, t, h, m)
                        mm(p[:, 0:st.NK], qT[64 * m:64 * m + 64, h, t * P:(t + 1) * P], kT[64 * m:64 * m + 64, h, 0:st.NK],
                           start=True, stop=True).then_inc(*made("s", k, t, h, m))

                scores_of(*heads[0])
                for i, (t, h) in enumerate(heads):
                    if i + 1 < len(heads):
                        scores_of(*heads[i + 1])
                    p = job(pe, "wT", k, t, h)
                    pe.wait_ge(*after("aw", k, t, h))
                    for kt in range(st.NK // P):
                        ins = tr(p[:, kt * P:(kt + 1) * P], prob[i % 2][0][:, kt * P:(kt + 1) * P], ident)
                    ins.then_inc(*made("wT", k, t, h))
                    p = job(pe, "o", k, t, h)
                    pe.wait_ge(*taken("wT", k, t, h))
                    for kt in range(st.NK // P):
                        v = v_nat[kt] if kt < T else v_cached
                        ins = mm(p[:, 0:P], wT[i % 2][:, kt * P:(kt + 1) * P], v[:, h * P:(h + 1) * P],
                                 start=(kt == 0), stop=(kt == st.NK // P - 1))
                    ins.then_inc(*made("o", k, t, h))
                    if t == 0 and h < ATT_HEADS - 1:
                        modulate_at(st, ("head", h))
                    if h == ATT_HEADS - 1:
                        p = job(pe, "oT", k, t)
                        pe.wait_ge(*after("o_n", k, t))
                        for b in range(4):
                            ins = tr(p[:, b * P:(b + 1) * P], o_nat[:, b * P:(b + 1) * P], ident)
                        ins.then_inc(*made("oT", k, t))
                pe.wait_ge(*taken("oT", k, T - 1))
                for cc in range(2):
                    pe.wait_ge(*chunk_landed("wo", k, cc))
                    for t in range(T):
                        p = job(pe, "wo", k, t, cc)
                        for b in range(DB):
                            ins = mm(p[:, :], catT[:, b, t * P:(t + 1) * P], chunk("wo", k, cc)[:, b, :],
                                     start=(b == 0), stop=(b == DB - 1))
                        ins.then_inc(*made("wo", k, t, cc))
                pe.wait_ge(*after("keys_in", k))
                for i in range(4):
                    p = job(pe, "kt", k, i)
                    for j in range(4):
                        b = 4 * i + j
                        ins = tr(p[:, j * P:(j + 1) * P], keys_nat[:, b * P:(b + 1) * P], ident)
                    ins.then_inc(*made("kt", k, i))
                turn_h(st, 1)
                pe.wait_ge(*taken("hT2", k, T - 1, 1))
                for b in range(16):
                    p = job(pe, "pq", k, b)
                    if b % 4 == 0:
                        pe.wait_ge(*chunk_landed("wq", k, b // 4))
                    for kb in range(DB):
                        ins = mm(p[:, 0:N], chunk("wq", k, b // 4)[:, kb, (b % 4) * P:(b % 4 + 1) * P], hT[1][:, kb, 0:N],
                                 start=(kb == 0), stop=(kb == DB - 1))
                    ins.then_inc(*made("pq", k, b))
                pe.wait_ge(*taken("pq", k, 15))
                for t in range(T):
                    for i in range(4):
                        p = job(pe, "ps", k, t, i)
                        for j in range(4):
                            b = 4 * i + j
                            key = (b % 2) * PEER_HEADS + b // 2
                            ins = mm(p[:, j * P:(j + 1) * P], pqT[:, b, t * P:(t + 1) * P], keysT[:, key * P:(key + 1) * P],
                                     start=True, stop=True)
                        ins.then_inc(*made("ps", k, t, i))
                modulate_at(st, "late")

            for st in steps:
                if st.first:
                    modulation(st.layer, MOD_ORDER[:4])
                dense(st)

        @block.scalar
        def _(act):
            A = nc.scalar.activation

            def take_row(layer, j):
                if j not in MOD_SCALES:
                    act.wait_ge(*full("mod", layer, j))
                    act.wait_ge(*after("row_stored", layer, MOD_ORDER[MOD_ORDER.index(j) - 1]))
                    A(mod_row[0:2, :], bank("mod", layer, j)[0:2, :], ACT.Copy).then_inc(*take("mod", layer, j))

            def modulation(layer):
                for j in MOD_ORDER[:4]:
                    take_row(layer, j)
                    yield ("mod", j)

            def modulate_at(st, point):
                if st.first:
                    for j in MOD_AT[point]:
                        take_row(st.layer, j)

            def carry(dst, src, *key, scale=1.0):
                act.wait_ge(*full(*key))
                A(dst, src, ACT.Copy, scale=scale).then_inc(*take(*key))

            def square(st, which):
                for t in range(st.T):
                    if which == 0:
                        if st.k < 2:
                            act.wait_ge(*after("x_in", 1))
                        else:
                            act.wait_ge(*after("x_new", st.k - 2, t))
                    else:
                        act.wait_ge(*after("x_mid", st.k, t))
                    A(hn[st.X + t][:, :], x[st.X + t][:, :], ACT.Square, accum_out=ss[:, t:t + 1])\
                        .then_inc(*mark("ss", st.k, which, t))

            def turn_h(st, which):
                name = ("hT1", "hT2")[which]
                for t in range(st.T):
                    for half in range(2):
                        carry(hT[which][:, 4 * half:4 * half + 4, t * P:(t + 1) * P],
                              bank(name, st.k, t, half)[:, :].rearrange("p (b n) -> p b n", b=4), name, st.k, t, half)

            def dense(st):
                k, T, N = st.k, st.T, st.N
                square(st, 0)
                yield "start"
                if st.first:
                    carry(columns, bank("par", st.layer)[:, 0:11], "par", st.layer)
                turn_h(st, 0)
                if k and st.lat:
                    act.wait_ge(*after("newv", st.layer))
                for name, where_to in (("q", 0), ("k", 512)):
                    for t in range(T):
                        carry(qk[t][:, where_to:where_to + 512], bank(name, k, t)[:, :], name, k, t)
                for t in range(T):
                    carry(v_nat[t], bank("v", k, t)[:, :], "v", k, t)
                for t in range(T):
                    carry(dtraw[:, 8 * t:8 * t + 8], bank("dt", k, t)[:, 0:8], "dt", k, t)
                for b in (4, 5, 0, 1, 2, 3):
                    carry(xraw[:, b, 2:2 + N], bank("xb", k, b)[:, 0:N], "xb", k, b)
                for t in range(T):
                    carry(pz[t], bank("pz", k, t)[:, :], "pz", k, t)
                if st.first:
                    act.wait_ge(*after("par_in", st.layer))
                    A(a_log, a_log, ACT.Exp).then_inc(*mark("par_ready", st.layer))
                    act.wait_ge(*after("par_lam", st.layer))
                    A(dot2[:, 0:2], dot2[:, 0:2], ACT.Exp).then_inc(*mark("lam", st.layer))
                yield "rope"
                act.wait_ge(*after("dt_abs", k))
                A(dt_u[:, 0:8 * T], dt_u[:, 0:8 * T], ACT.Exp, scale=-1.0).then_inc(*mark("dt_exp", k))
                act.wait_ge(*after("dt_sum", k))
                A(dt_u[:, 32:32 + 8 * T], dt_u[:, 16:16 + 8 * T], ACT.Ln).then_inc(*mark("dt_ln", k))
                act.wait_ge(*after("nacs", k))
                A(cumsum[:, 0:24 * T], cumsum[:, 0:24 * T], ACT.Exp).then_inc(*mark("decays", k))
                yield "dt"
                for t in range(T):
                    for side, dst in enumerate((qT, kT)):
                        carry(dst[:, :, t * P:(t + 1) * P],
                              bank("qkT", k, t, side)[:, :].rearrange("p (h n) -> p h n", h=4), "qkT", k, t, side)
                if st.lat:
                    carry(kT[:, :, N:N + P], bank("kc", k)[:, :].rearrange("p (h n) -> p h n", h=4), "kc", k)
                yield "conv"
                for pair in range(2):
                    carry(pooledT[:, pair, 0:N], bank("pl", k, pair)[:, 0:N], "pl", k, pair)
                if not st.lat:
                    act.wait_ge(*after("newk", st.layer))
                for pair in range(2):
                    carry(catT[:, pair, 0:N], bank("pm", k, pair)[:, 0:N], "pm", k, pair, scale=pool_s[:, pair:pair + 1])
                modulate_at(st, "summed")
                act.wait_ge(*after("conv_sum", k))
                A(conv[:, :, 0:N], conv[:, :, 0:N], ACT.Silu).then_inc(*mark("conv", k))
                for t in range(T):
                    A(pz[t][:, 256:512], pz[t][:, 256:512], ACT.Silu).then_inc(*mark("silu_z", k, t))
                for t in range(T):
                    carry(nat[t], bank("xbn", k, t)[:, :], "xbn", k, t)
                if st.lat:
                    carry(enter0, bank("init", k)[:, :], "init", k)
                yield "xw"
                if not st.lat:
                    carry(enter0, bank("st", k)[:, :], "st", k)
                modulate_at(st, "states")
                for t in range(T):
                    for d in range(2):
                        act.wait_ge(*full("seg", k, t, d))
                        if d == 0 and t:
                            act.wait_ge(*after("M", k, t - 1))
                        for h in range(4):
                            o = (4 * d + h) * P
                            ins = A(decay[:, o:o + P], bank("seg", k, t, d)[:, h * P:(h + 1) * P], ACT.Exp,
                                    bias=dt_end[:, 8 * t + 4 * d + h:8 * t + 4 * d + h + 1])
                        ins.then_inc(*take("seg", k, t, d))
                    yield ("seg", t)
                modulate_at(st, "scanned")
                for t in range(T):
                    for b in range(2):
                        act.wait_ge(*full("yT", k, t))
                        ins = A(catT[:, 2 + b, t * P:(t + 1) * P], bank("yT", k, t)[:, b * P:(b + 1) * P], ACT.Copy,
                                scale=y_w[:, b:b + 1])
                    ins.then_inc(*take("yT", k, t))
                yield "y"
                heads = [(t, h) for t in range(T) for h in range(ATT_HEADS)]

                def exps(i):
                    t, h = heads[i]
                    act.wait_ge(*after("mx", k, t, h))
                    for m in range(2):
                        A(prob[i % 2][m][:, 0:st.NK], bank("s", k, t, h, m)[:, 0:st.NK], ACT.Exp,
                          bias=mx[i % 2][:, m:m + 1], scale=ATT_SCALE,
                          accum_out=sums[i % 2][:, m:m + 1]).then_inc(*take("s", k, t, h, m))

                exps(0)
                for i, (t, h) in enumerate(heads):
                    if i + 1 < len(heads):
                        exps(i + 1)
                    carry(wT[i % 2][:, 0:st.NK], bank("wT", k, t, h)[:, 0:st.NK], "wT", k, t, h)
                    if h == 0 and t:
                        act.wait_ge(*full("oT", k, t - 1))
                    carry(o_nat[:, h * P:(h + 1) * P], bank("o", k, t, h)[:, 0:P], "o", k, t, h)
                    if t == 0 and h < ATT_HEADS - 1:
                        modulate_at(st, ("head", h))
                    if h == ATT_HEADS - 1:
                        act.wait_ge(*full("oT", k, t))
                        A(catT[:, 4:8, t * P:(t + 1) * P], bank("oT", k, t)[:, :].rearrange("p (b n) -> p b n", b=4),
                          ACT.Copy, scale=subln_s).then_inc(*take("oT", k, t))
                    if h % 2 == 1:
                        yield ("att", 4 * t + h)
                for i in range(4):
                    carry(keysT[:, i * 512:(i + 1) * 512], bank("kt", k, i)[:, :], "kt", k, i)
                square(st, 1)
                yield "mid"
                turn_h(st, 1)
                for b in range(16):
                    carry(pqT[:, b, 0:N], bank("pq", k, b)[:, 0:N], "pq", k, b)
                for t in range(T):
                    for i in range(4):
                        if t and i == 0:
                            act.wait_ge(*after("picked", k, t - 1))
                        carry(scores[:, i * 512:(i + 1) * 512], bank("ps", k, t, i)[:, :], "ps", k, t, i)
                    yield ("ps", t)
                    act.wait_ge(*after("topk_diff", k, t))
                    A(best_v, best_v, ACT.Exp).then_inc(*mark("topk_exp", k, t))
                    yield ("exp", t)
                modulate_at(st, "late")

            def gelu(k, t):
                at = (steps[k].X + t) * PICKS
                act.wait_ge(*after("act_done", k, t))
                A(dots[:, at:at + PICKS], dots[:, at:at + PICKS], ACT.Gelu_apprx_tanh).then_inc(*mark("gelu", k, t))

            act.wait_ge(*full("cond"))
            A(cond[:, :], bank("cond")[:, 0:16], ACT.Silu).then_inc(*take("cond"))
            run_beside(steps, modulation, dense, lambda k, kind, t, span: gelu(k, t) if kind == 2 else None, False)

        @block.vector
        def _(dve):
            V = nc.vector
            done = [0]

            def d(ins):
                done[0] += 1
                ins.then_inc(sems["v_step"], 1)

            def settle():
                dve.wait_ge(sems["v_step"], done[0])

            def inverse_rms(out, sq, n):
                w = out.shape[1]
                mean, by = root[:, 0:w], root[:, 4:4 + w]
                d(V.tensor_scalar(mean, sq, 1.0 / n, EPS, ALU.mult, ALU.add))
                settle()
                d(V.tensor_single_scalar(root_bits[:, 0:w], mean.bitcast(U32), 1, ALU.logical_shift_right))
                settle()
                d(V.tensor_scalar(out.bitcast(U32), root_bits[:, 0:w], -1.0, float(0x5F3759DF), ALU.mult, ALU.add))
                settle()
                for _ in range(4):
                    if w == 1:
                        d(V.scalar_tensor_tensor(by, out, mean, out, ALU.mult, ALU.mult))
                    else:
                        d(V.tensor_tensor(by, out, out, ALU.mult))
                        settle()
                        d(V.tensor_tensor(by, by, mean, ALU.mult))
                    settle()
                    d(V.tensor_scalar(by, by, -0.5, 1.5, ALU.mult, ALU.add))
                    settle()
                    d(V.tensor_tensor(out, out, by, ALU.mult))
                    settle()

            def take_row(layer, j):
                if j in MOD_SCALES:
                    dve.wait_ge(*full("mod", layer, j))
                    dve.wait_ge(*after("nw_in", layer, j))
                    n = MOD_ORDER.index(j)
                    if n or layer:
                        dve.wait_ge(*after("row_stored", *((layer, MOD_ORDER[n - 1]) if n else (layer - 1, MOD_ORDER[-1]))))
                    V.scalar_tensor_tensor(mod_row[0:2, :], bank("mod", layer, j)[0:2, :], 1.0, mod_nw[0:2, :],
                                           ALU.add, ALU.mult).then_inc(*take("mod", layer, j))

            def modulation(layer):
                for j in MOD_ORDER[:4]:
                    take_row(layer, j)
                    yield ("mod", j)

            def modulate_at(st, point):
                if st.first:
                    for j in MOD_AT[point]:
                        take_row(st.layer, j)

            def modulate(st, which):
                name = ("h1", "h2")[which]
                for t in range(st.T):
                    dve.wait_ge(*after("ss", st.k, which, t))
                    inverse_rms(rstd[:, t:t + 1], ss[:, t:t + 1], D)
                    h = hn[st.X + t][:, :]
                    dve.wait_ge(*after("mod_a", st.k, 4 if which else 1))
                    d(V.scalar_tensor_tensor(h, x[st.X + t][:, :], rstd[:, t:t + 1], mod_a[:, :], ALU.mult, ALU.mult))
                    settle()
                    dve.wait_ge(*after("mod_b", st.k, 3 if which else 0))
                    V.tensor_tensor(h, h, mod_b[:, :], ALU.add).then_inc(*mark(name, st.k, t))

            def rounds(values, n, width, top, index, t, at):
                for r in range(2):
                    for b in range(n):
                        d(V.max(top[:, b * TOPK + 8 * r:b * TOPK + 8 * r + 8], values[:, b * width:(b + 1) * width]))
                    settle()
                    for b in range(n):
                        d(V.max_index(index[:, b * TOPK + 8 * r:b * TOPK + 8 * r + 8],
                                      top[:, b * TOPK + 8 * r:b * TOPK + 8 * r + 8], values[:, b * width:(b + 1) * width]))
                    settle()
                    if r == 0:
                        for b in range(n):
                            d(V.match_replace(values[:, b * width:(b + 1) * width], top[:, b * TOPK:b * TOPK + 8],
                                              values[:, b * width:(b + 1) * width], LOWEST))
                        settle()
                    yield ("choose", t, at + r)

            def choose(st, t):
                k = st.k
                for i in range(4):
                    dve.wait_ge(*taken("ps", k, t, i))
                yield from rounds(scores, 2 * PEER_HEADS, P, top_v, top_i, t, 0)
                d(V.tensor_copy(top_f, top_i))
                tv = top_v.rearrange("p (h m a) -> p h m a", h=PEER_HEADS, m=2)
                cd, first = cand.rearrange("p (h n) -> p h n", h=PEER_HEADS), 0
                for row, n, m in CELLS:
                    wide = [P, PEER_HEADS, n, m]
                    d(V.tensor_tensor(cd[:, :, first:first + n * m].rearrange("p h (a b) -> p h a b", b=m),
                                      tv[:, :, 0, row:row + n].unsqueeze(3).broadcast_to(wide),
                                      tv[:, :, 1, 0:m].unsqueeze(2).broadcast_to(wide), ALU.add))
                    first += n * m
                settle()
                yield from rounds(cand, PEER_HEADS, PACKED, best_v, best_p, t, 2)
                d(V.tensor_copy(packed_p, best_p))
                settle()
                d(V.tensor_copy(place, packed_p))
                first = 0
                for row, n, m in CELLS:
                    starts = [first + m * i for i in range(1, n + (row + n < TOPK))]
                    first += n * m
                    if m == TOPK or not starts:
                        continue
                    settle()
                    if m == 1:
                        d(V.tensor_scalar(passed, packed_p, float(starts[0] - 1), 0.0, ALU.subtract, ALU.max))
                    else:
                        d(V.tensor_single_scalar(passed, packed_p, float(starts[0]), ALU.is_ge))
                        for at in starts[1:]:
                            settle()
                            d(V.scalar_tensor_tensor(passed, packed_p, float(at), passed, ALU.is_ge, ALU.add))
                    settle()
                    d(V.scalar_tensor_tensor(place, passed, float(TOPK - m), place, ALU.mult, ALU.add))
                settle()
                d(V.tensor_copy(best_p, place))
                settle()
                d(V.tensor_single_scalar(half_p, best_p, 4, ALU.logical_shift_right))
                settle()
                d(V.tensor_copy(half_f[0], half_p))
                settle()
                d(V.tensor_single_scalar(half_p, best_p, 15, ALU.bitwise_and))
                settle()
                d(V.tensor_copy(half_f[1], half_p))
                settle()
                tf = top_f.rearrange("p (h m a) -> p h m a", h=PEER_HEADS, m=2)
                wide = [P, PEER_HEADS, TOPK, TOPK]
                for m in range(2):
                    hm = hot[m].rearrange("p (h k a) -> p h k a", h=PEER_HEADS, k=TOPK)
                    rank = half_f[m].rearrange("p (h k) -> p h k", h=PEER_HEADS).unsqueeze(3).broadcast_to(wide)
                    iota = c("iota").unsqueeze(1).unsqueeze(1).broadcast_to(wide)
                    d(V.tensor_tensor(hm, rank, iota, ALU.is_equal))
                    yield ("choose", t, 4 + m)
                settle()
                for m in range(2):
                    hm = hot[m].rearrange("p (h k a) -> p h k a", h=PEER_HEADS, k=TOPK)
                    d(V.tensor_tensor(hm, hm, tf[:, :, m, :].unsqueeze(2).broadcast_to(wide), ALU.mult))
                settle()
                yield ("choose", t, 6)
                for m in range(2):
                    d(V.tensor_reduce(half_f[m], hot[m].rearrange("p (q a) -> p q a", a=TOPK), AX_X, ALU.add))
                settle()
                at = (st.X + t) * PICKS
                d(V.tensor_scalar(half_f[0], half_f[0], float(P), float(st.layer * EXPERTS), ALU.mult, ALU.add))
                settle()
                d(V.tensor_tensor(idx[:, at:at + PICKS], half_f[0], half_f[1], ALU.add))
                bv = best_v.rearrange("p (h k) -> p h k", h=PEER_HEADS)
                d(V.tensor_copy(e_sum, bv[:, :, 0]))
                settle()
                V.tensor_tensor(bv, bv, e_sum.unsqueeze(2).broadcast_to([P, PEER_HEADS, TOPK]), ALU.subtract)\
                    .then_inc(*mark("topk_diff", k, t))
                yield ("choose", t, 7)
                dve.wait_ge(*after("topk_exp", k, t))
                d(V.tensor_reduce(e_sum, bv, AX_X, ALU.add))
                settle()
                d(V.reciprocal(e_sum, e_sum))
                settle()
                V.tensor_tensor(gates[:, at:at + PICKS].rearrange("p (h k) -> p h k", h=PEER_HEADS), bv,
                                e_sum.unsqueeze(2).broadcast_to([P, PEER_HEADS, TOPK]), ALU.mult)\
                    .then_inc(*mark("picked", k, t))
                dve.wait_ge(*after("picked", k, t))
                yield ("exp", t)

            def dense(st):
                k, T, N = st.k, st.T, st.N
                yield "start"
                modulate(st, 0)
                yield "h1"
                if st.first:
                    dve.wait_ge(*after("par_in", st.layer))
                    pr = lam_in.rearrange("p (a b) -> p a b", a=4)
                    d(V.tensor_tensor_reduce(pr[:, 0, :], pr[:, 0, :], pr[:, 1, :], 1.0, 0.0, ALU.mult, ALU.add, dot2[:, 0:1]))
                    d(V.tensor_tensor(d_sum, d_skip[:, 0:4], d_skip[:, 4:8], ALU.add))
                    V.tensor_tensor_reduce(pr[:, 2, :], pr[:, 2, :], pr[:, 3, :], 1.0, 0.0, ALU.mult, ALU.add, dot2[:, 1:2])\
                        .then_inc(*mark("par_lam", st.layer))
                d(V.memset(xraw[:, :, 0:2], 0.0))
                d(V.memset(xraw[:, :, N + 2:N + 4], 0.0))
                if st.lat:
                    for t in range(T):
                        dve.wait_ge(*taken("q", k, t))
                        dve.wait_ge(*taken("k", k, t))
                        q4 = qk[t].rearrange("p (u x s i) -> p u x s i", u=16, x=2, s=2)
                        r4 = rope_tmp.rearrange("p (u x s i) -> p u x s i", u=16, x=2, s=2)
                        sin = c("sin", 64 * t, 64).rearrange("p (x s i) -> p x s i", x=2, s=2)
                        for s in range(2):
                            d(V.tensor_tensor(r4[:, :, :, s, :], q4[:, :, :, 1 - s, :],
                                              sin[:, :, s, :].unsqueeze(1).broadcast_to([P, 16, 2, 16]), ALU.mult))
                        settle()
                        q3 = qk[t].rearrange("p (u i) -> p u i", u=16)
                        d(V.tensor_tensor(q3, q3, c("cos", 64 * t, 64).unsqueeze(1).broadcast_to([P, 16, 64]), ALU.mult))
                        settle()
                        V.tensor_tensor(qk[t], qk[t], rope_tmp, ALU.add).then_inc(*mark("rope", k, t))
                        dve.wait_ge(*after("rope", k, t))
                if st.first:
                    dve.wait_ge(*taken("par", st.layer))
                    dve.wait_ge(*after("par_ready", st.layer))
                    d(V.tensor_scalar(a_log, a_log, -1.0, None, ALU.mult))
                    dve.wait_ge(*after("lam", st.layer))
                    d(V.tensor_tensor(lam, dot2[:, 0:1], dot2[:, 1:2], ALU.subtract))
                    settle()
                    d(V.scalar_tensor_tensor(lam, lam, -1.0, c("lam", st.layer, 1), ALU.mult, ALU.subtract))
                    d(V.tensor_tensor(subln_s, subln, c("lam", DEPTH + st.layer, 1), ALU.mult))
                    settle()
                yield "rope"
                n = 8 * T
                u, w1, ln = dt_u[:, 0:n], dt_u[:, 16:16 + n], dt_u[:, 32:32 + n]
                dv, tmp = dt[:, 0:n], dt_tmp[:, 0:n]
                dve.wait_ge(*taken("dt", k, T - 1))
                d(V.tensor_tensor(dv.rearrange("p (t h) -> p t h", h=8), dtraw[:, 0:n].rearrange("p (t h) -> p t h", h=8),
                                  dt_bias.unsqueeze(1).broadcast_to([P, T, 8]), ALU.add))
                settle()
                d(V.tensor_scalar(u, dv, -1.0, None, ALU.mult))
                settle()
                V.tensor_tensor(u, u, dv, ALU.max).then_inc(*mark("dt_abs", k))
                dve.wait_ge(*after("dt_exp", k))
                V.tensor_scalar(w1, u, 1.0, None, ALU.add).then_inc(*mark("dt_sum", k))
                dve.wait_ge(*after("dt_ln", k))
                d(V.tensor_scalar(w1, w1, 1.0, None, ALU.subtract))
                settle()
                d(V.tensor_scalar(tmp, w1, 0.0, None, ALU.is_equal))
                settle()
                d(V.tensor_tensor(w1, w1, tmp, ALU.add))
                d(V.tensor_tensor(ln, ln, u, ALU.mult))
                d(V.tensor_tensor(tmp, tmp, u, ALU.mult))
                d(V.tensor_scalar(dv, dv, 0.0, None, ALU.max))
                settle()
                d(V.reciprocal(w1, w1))
                d(V.tensor_tensor(dv, dv, tmp, ALU.add))
                settle()
                d(V.tensor_tensor(ln, ln, w1, ALU.mult))
                settle()
                d(V.tensor_tensor(dv, dv, ln, ALU.add))
                settle()
                V.tensor_tensor(dta[:, 0:n].rearrange("p (t h) -> p t h", h=8), dv.rearrange("p (t h) -> p t h", h=8),
                                a_log.unsqueeze(1).broadcast_to([P, T, 8]), ALU.mult).then_inc(*mark("dta", k))
                dve.wait_ge(*full("cum", k))
                cp = bank("cum", k)[:, 0:24 * T].rearrange("p (t n) -> p t n", t=T)
                cs = cumsum[:, 0:24 * T].rearrange("p (t n) -> p t n", t=T)
                ne = dt_end[:, 0:n].rearrange("p (t n) -> p t n", t=T)
                V.tensor_copy(cs[:, :, 0:16], cp[:, :, 0:16]).then_inc(*take("cum", k))
                dve.wait_ge(*taken("cum", k))
                d(V.tensor_scalar(ne, cs[:, :, 0:8], -1.0, None, ALU.mult))
                V.tensor_tensor(cs[:, :, 16:24], cs[:, :, 8:16], cs[:, :, 0:8], ALU.subtract).then_inc(*mark("nacs", k))
                dve.wait_ge(*after("decays", k))
                d(V.tensor_tensor(dt_tmp[:, 0:n].rearrange("p (t n) -> p t n", t=T), dv.rearrange("p (t n) -> p t n", t=T),
                                  cs[:, :, 16:24], ALU.mult))
                settle()
                yield "dt"
                for b in range(CONV_BLOCKS):
                    dve.wait_ge(*taken("xb", k, b))
                settle()
                for j in range(TAPS):
                    for b in range(CONV_BLOCKS):
                        o, src, w = conv[:, b, 0:N], xraw[:, b, j:j + N], conv_w[:, b, j:j + 1]
                        if j == 0:
                            d(V.tensor_scalar(o, src, w, conv_b[:, b:b + 1], ALU.mult, ALU.add))
                        elif j == TAPS - 1 and b == CONV_BLOCKS - 1:
                            V.scalar_tensor_tensor(o, src, w, o, ALU.mult, ALU.add).then_inc(*mark("conv_sum", k))
                        else:
                            d(V.scalar_tensor_tensor(o, src, w, o, ALU.mult, ALU.add))
                    settle()
                yield "conv"
                for s in range(2):
                    t = s if st.lat else 0
                    dve.wait_ge(*taken("xbn", k, t))
                    V.tensor_tensor(xw[:, s * 256:(s + 1) * 256].rearrange("p (h n) -> p h n", h=4),
                                    nat[t][:, 0:256].rearrange("p (h n) -> p h n", h=4),
                                    dt_tmp[:, 8 * t + 4 * s:8 * t + 4 * s + 4].unsqueeze(2).broadcast_to([P, 4, 64]),
                                    ALU.mult).then_inc(*mark("xw", k, s))
                if st.lat:
                    dve.wait_ge(*taken("init", k))
                    for s in range(2):
                        d(V.tensor_tensor(enter1[:, s * 256:(s + 1) * 256].rearrange("p (h n) -> p h n", h=4),
                                          enter0[:, s * 256:(s + 1) * 256].rearrange("p (h n) -> p h n", h=4),
                                          cs[:, s, 8 + 4 * s:12 + 4 * s].unsqueeze(2).broadcast_to([P, 4, 64]), ALU.mult))
                    settle()
                    dve.wait_ge(*full("st", k))
                    V.tensor_tensor(enter1, enter1, bank("st", k)[:, :], ALU.add).then_inc(*take("st", k))
                    dve.wait_ge(*taken("st", k))
                yield "xw"
                for t in range(T):
                    if t:
                        dve.wait_ge(*full("seg", k, t - 1, 1))
                    V.tensor_copy(dta_rep.rearrange("p (h n) -> p h n", h=8),
                                  dta[:, 8 * t:8 * t + 8].unsqueeze(2).broadcast_to([P, 8, P])).then_inc(*mark("rep", k, t))
                    yield ("decay", t)
                    for s in range(2):
                        dve.wait_ge(*taken("seg", k, t, s))
                    dec = decay.rearrange("p (h n) -> p h n", h=8)
                    d(V.tensor_tensor(dec, dec, dt[:, 8 * t:8 * t + 8].unsqueeze(2).broadcast_to([P, 8, P]), ALU.mult))
                    settle()
                    if t:
                        dve.wait_ge(*full("y", k, t - 1))
                    d(V.tensor_tensor(mixed, decay[:, 0:512], decay[:, 512:1024], ALU.add))
                    settle()
                    dve.wait_ge(*full("cb", k, t))
                    m4 = mixed.rearrange("p (g r n) -> p g r n", g=2, r=2)
                    cb = bank("cb", k, t)[:, 0:256].rearrange("p (g n) -> p g n", g=2).unsqueeze(2).broadcast_to([P, 2, 2, P])
                    d(V.tensor_tensor(m4, m4, cb, ALU.mult))
                    settle()
                    V.memset(dot2[:, 2:3], 0.0).then_inc(*take("cb", k, t))
                    V.memset(dot2[:, 3:4], 0.0).then_inc(*mark("M", k, t))
                    y3 = y_nat[t].rearrange("p (h n) -> p h n", h=4)
                    d(V.tensor_tensor(y3, nat[t][:, 0:256].rearrange("p (h n) -> p h n", h=4),
                                      d_sum.unsqueeze(2).broadcast_to([P, 4, 64]), ALU.mult))
                    settle()
                    if st.lat:
                        dve.wait_ge(*full("yo", k, t))
                        V.tensor_tensor(decay[:, 0:512].rearrange("p (h n) -> p h n", h=8),
                                        bank("yo", k, t)[:, :].rearrange("p (h n) -> p h n", h=8),
                                        cs[:, t, 0:8].unsqueeze(2).broadcast_to([P, 8, 64]), ALU.mult)\
                            .then_inc(*take("yo", k, t))
                        dve.wait_ge(*taken("yo", k, t))
                        d(V.tensor_tensor(y_nat[t], y_nat[t], decay[:, 0:256], ALU.add))
                        settle()
                        d(V.tensor_tensor(y_nat[t], y_nat[t], decay[:, 256:512], ALU.add))
                        settle()
                    dve.wait_ge(*full("y", k, t))
                    V.tensor_tensor(y_nat[t], y_nat[t], bank("y", k, t)[:, 0:256], ALU.add).then_inc(*take("y", k, t))
                    dve.wait_ge(*taken("y", k, t))
                    dve.wait_ge(*after("silu_z", k, t))
                    d(V.tensor_tensor(y_nat[t], y_nat[t], pz[t][:, 256:512], ALU.mult))
                    settle()
                    d(V.tensor_tensor_reduce(pz[t][:, 256:512], y_nat[t], y_nat[t], 1.0, 0.0, ALU.mult, ALU.add, ss[:, 2:3]))
                    settle()
                    inverse_rms(rstd[:, 2:3], ss[:, 2:3], 256)
                    V.tensor_scalar(y_nat[t], y_nat[t], rstd[:, 2:3], None, ALU.mult).then_inc(*mark("y_n", k, t))
                    yield ("seg", t)
                modulate_at(st, "scanned")
                yield "y"
                heads = [(t, h) for t in range(T) for h in range(ATT_HEADS)]

                def row_max(i):
                    t, h = heads[i]
                    for m in range(2):
                        dve.wait_ge(*full("s", k, t, h, m))
                        d(V.reduce_max(mx[i % 2][:, m:m + 1], bank("s", k, t, h, m)[:, 0:st.NK], AX_X))
                    settle()
                    V.tensor_scalar(mx[i % 2], mx[i % 2], -ATT_SCALE, None, ALU.mult).then_inc(*mark("mx", k, t, h))

                row_max(0)
                for i, (t, h) in enumerate(heads):
                    if i + 1 < len(heads):
                        row_max(i + 1)
                    yield ("head", i)
                    for m in range(2):
                        dve.wait_ge(*taken("s", k, t, h, m))
                    sm = sums[i % 2]
                    d(V.reciprocal(sm, sm))
                    settle()
                    d(V.tensor_scalar(sm[:, 1:2], sm[:, 1:2], lam, None, ALU.mult))
                    p0, p1 = (prob[i % 2][m][:, 0:st.NK] for m in range(2))
                    d(V.tensor_scalar(p0, p0, sm[:, 0:1], None, ALU.mult))
                    settle()
                    V.scalar_tensor_tensor(p0, p1, sm[:, 1:2], p0, ALU.mult, ALU.add).then_inc(*mark("aw", k, t, h))
                    if t == 0 and h < ATT_HEADS - 1:
                        modulate_at(st, ("head", h))
                    if h == ATT_HEADS - 1:
                        dve.wait_ge(*taken("o", k, t, h))
                        o3 = o_nat.rearrange("p (h n) -> p h n", h=4)
                        d(V.tensor_tensor(mixed, o_nat, o_nat, ALU.mult))
                        settle()
                        d(V.tensor_reduce(ss[:, 0:4], mixed.rearrange("p (h n) -> p h n", h=4), AX_X, ALU.add))
                        settle()
                        inverse_rms(rstd[:, 0:4], ss[:, 0:4], P)
                        V.tensor_tensor(o3, o3, rstd[:, 0:4].unsqueeze(2).broadcast_to([P, 4, P]), ALU.mult)\
                            .then_inc(*mark("o_n", k, t))
                    if h % 2 == 1:
                        yield ("att", 4 * t + h)
                yield "wo"
                dve.wait_ge(*after("mod_g1", k, 2))
                for cc in range(2):
                    for t in range(T):
                        tmp = mixed if (cc * T + t) % 2 == 0 else xw
                        g = mod_g1[:, cc * CHUNK:(cc + 1) * CHUNK]
                        xt = x[st.X + t][:, cc * CHUNK:(cc + 1) * CHUNK]
                        dve.wait_ge(*full("wo", k, t, cc))
                        V.tensor_tensor(tmp, bank("wo", k, t, cc)[:, :], g, ALU.mult).then_inc(*take("wo", k, t, cc))
                        dve.wait_ge(*taken("wo", k, t, cc))
                        if cc:
                            V.tensor_tensor(xt, xt, tmp, ALU.add).then_inc(*mark("x_mid", k, t))
                        else:
                            d(V.tensor_tensor(xt, xt, tmp, ALU.add))
                yield "mid"
                modulate(st, 1)
                yield ("ps", 0)
                for t in range(T):
                    if t:
                        yield ("ps", t)
                    yield from choose(st, t)

            def gather(k, which, t, part):
                st = steps[k]
                n = st.X + t
                base, col = pass_base[k, which if which < 2 else 1, t], n * PICKS
                if which == 0:
                    lo, hi = part
                    with dve.Fori(lo, hi) as turn:
                        for r in range(PART):
                            slot = r % RING
                            dve.wait_ge(row_landed[slot], turn * (16 * PART // RING) + (16 * (base // RING + r // RING + 1)))
                            V.tensor_tensor_reduce(rows[slot][:, :], rows[slot][:, :], hn[n][:, :], 1.0, 0.0, ALU.mult,
                                                   ALU.add, dots_now[:, r:r + 1]).then_inc(row_used, 1)
                        dve.wait_ge(row_used, turn * PART + (RING + base + PART))
                        V.tensor_copy(dots[:, bass.ds(turn * PART + col, PART)], dots_now[:, :])\
                            .then_inc(sems["dots_copied"], 1)
                        dve.wait_ge(sems["dots_copied"], turn + (dots_base[k, t] + 1))
                    if hi == PICKS // PART:
                        V.memset(dot2[:, 2:3], 0.0).then_inc(*mark("act_done", k, t))
                elif which == 2:
                    dve.wait_ge(*after("gelu", k, t))
                    d(V.tensor_tensor(picks_w[:, col:col + PICKS], dots[:, col:col + PICKS], gates[:, col:col + PICKS], ALU.mult))
                    settle()
                else:
                    lo, hi = part
                    if lo == 0:
                        for a in range(2):
                            d(V.memset(acc[a][:, :], 0.0))
                        settle()
                    with dve.Fori(lo, hi) as turn:
                        for r in range(PART):
                            slot = r % RING
                            dve.wait_ge(row_used, turn * PART + (RING + base + r - 1))
                            dve.wait_ge(row_landed[slot], turn * (16 * PART // RING) + (16 * (base // RING + r // RING + 1)))
                            V.scalar_tensor_tensor(acc[r % 2][:, :], rows[slot][:, :],
                                                   picks_w[:, bass.ds(turn * PART + (col + r), 1)], acc[r % 2][:, :],
                                                   ALU.mult, ALU.add).then_inc(row_used, 1)
                    if hi == PICKS // PART:
                        dve.wait_ge(row_used, RING + base + PICKS)
                        d(V.tensor_tensor(acc[0][:, :], acc[0][:, :], acc[1][:, :], ALU.add))
                        settle()
                        dve.wait_ge(*after("mod_g2", k, 5))
                        d(V.tensor_tensor(acc[0][:, :], acc[0][:, :], mod_g2[st.s][:, :], ALU.mult))
                        settle()
                        V.tensor_tensor(x[n][:, :], x[n][:, :], acc[0][:, :], ALU.add).then_inc(*mark("x_new", k, t))
                        dve.wait_ge(*after("x_new", k, t))
                        if st.layer == DEPTH - 1:
                            d(V.tensor_tensor_reduce(acc[0][:, :], x[n][:, :], x[n][:, :], 1.0, 0.0, ALU.mult, ALU.add,
                                                     ss[:, 3:4]))
                            settle()
                            inverse_rms(rstd[:, 3:4], ss[:, 3:4], D)
                            dve.wait_ge(*after("fw_in", k))
                            V.scalar_tensor_tensor(x[n][:, :], x[n][:, :], rstd[:, 3:4], hn[st.X][:, :],
                                                   ALU.mult, ALU.mult).then_inc(*mark("y_ready", k, t))

            dots_base, n = {}, 0
            for st in steps:
                for t in range(st.T):
                    dots_base[st.k, t] = n
                    n += PICKS // PART
            dve.sem_inc(row_used, RING)
            dve.wait_ge(*after("consts_in"))
            run_beside(steps, modulation, dense, gather, True)

    assert sorted(map(str, took)) == sorted(map(str, numbers)), "each psum job is taken once"
    return numbers, M.reached


def pauses_of(st):
    names = []
    if st.first and st.k:
        names += [(("mod", j), True, 0.5) for j in MOD_ORDER[:4]]
    names += [("start", True, 0), ("h1", False, 6), ("rope", True, 1), ("dt", True, 2), ("conv", True, 1), ("xw", True, 0)]
    for t in range(st.T):
        names += [(("decay", t), False, 0.5), (("seg", t), True, 0.5)]
    names += [("y", True, 0.5)]
    for i in range(st.T * ATT_HEADS):
        names += [(("head", i), False, 1)]
        if i % 2 == 1:
            names += [(("att", i), True, 0)]
    names += [("wo", False, 2), ("mid", True, 0), (("ps", 0), True, 5)]
    for t in range(st.T):
        if t:
            names += [(("ps", t), True, 0)]
        names += [(("choose", t, i), False, 0.4) for i in range(8)]
        names += [(("exp", t), True, 0)]
    return names


def gather_plan(steps, k):
    st = steps[k - 1]
    turns = PICKS // PART
    todo = [(0, t, (i, i + 1)) for t in range(st.T) for i in range(turns)]
    todo += [(2, t, None) for t in range(st.T)]
    todo += [(1, t, (i, i + 1)) for t in range(st.T) for i in range(turns)]
    plan, done = {}, 0
    names = pauses_of(steps[k]) if k < len(steps) else []
    whole = sum(w for _, _, w in names)
    so_far = 0.0
    for name, common, weight in names:
        so_far += weight
        here = plan.setdefault(name, [])
        while todo and done < int(len(todo_all(st)) * so_far / whole):
            if todo[0][0] == 2 and not common:
                break
            here.append(todo.pop(0))
            done += 1
    plan[None] = todo
    for name in plan:
        plan[name] = joined(plan[name])
    return plan


def todo_all(st):
    return range(2 * st.T * (PICKS // PART) + st.T)


def joined(parts):
    out = []
    for kind, t, span in parts:
        if span and out and out[-1][0] == kind and out[-1][1] == t:
            out[-1] = (kind, t, (out[-1][2][0], span[1]))
        else:
            out.append((kind, t, span))
    return out


def run_beside(steps, modulation, dense, gather, everything):
    for k in range(len(steps) + 1):
        plan = gather_plan(steps, k) if k else {}

        def beside(name):
            for kind, t, span in plan.get(name, []):
                gather(k - 1, kind, t, span)

        if k < len(steps):
            names = [n for n, common, _ in pauses_of(steps[k]) if everything or common]
            seen = []
            if steps[k].first:
                for name in modulation(steps[k].layer):
                    if k:
                        seen.append(name)
                        beside(name)
            for name in dense(steps[k]):
                seen.append(name)
                beside(name)
            assert seen == names, (seen, names)
        beside(None)


INPUTS = ["x_prompt", "x_sample", "cache_attn_k", "cache_attn_v", "state_ssd_fwd", "state_ssd_bwd", "c", "c_ctx",
          "mod_w", "mod_b", "norm1_w", "norm2_w", "w_in", "pool_w", "pool_scale", "ssd_conv_w", "ssd_conv_b",
          "ssd_A_log", "ssd_dt_bias", "ssd_D", "ssd_norm_w", "attn_lambda", "attn_subln_w", "w_out", "peer_wq",
          "peer_keys", "peer_u", "peer_v", "final_norm_w"]
OUTPUTS = {"y_prompt": (1, 128, 1024), "y_sample": (1, 256, 1024), "new_k": (1, DEPTH, 128, 4, 128),
           "new_v": (1, DEPTH, 128, 4, 128), "new_f": (1, DEPTH, 4, 64, 128), "new_b": (1, DEPTH, 4, 64, 128)}


def declare(nc, arrays):
    io = {name: nc.dram_tensor(name + "_in", a.shape, F32, kind="ExternalInput").ap() for name, a in arrays.items()}
    for name, shape in OUTPUTS.items():
        io[name] = nc.dram_tensor(name + "_out", shape, F32, kind="ExternalOutput").ap()
    io["mod_scratch"] = nc.dram_tensor("mod_scratch", (DEPTH, 6, 2, D), F32, kind="Internal").ap()
    io["state_fwd"], io["state_bwd"] = io["state_ssd_fwd"], io["state_ssd_bwd"]
    for name in ("peer_u", "peer_v"):
        io[name] = io[name].rearrange("l e d -> (l e) d")
    return io


def kernel(**inputs):
    import concourse.bacc as bacc
    from concourse.bass_utils import run_bass_kernel_spmd

    where, const, band_lat, band_ctx = shape_constants()
    arrays = {name: np.ascontiguousarray(inputs[name]) for name in INPUTS}
    arrays |= {"const": const, "band_lat": band_lat, "band_ctx": band_ctx}
    known = None
    for _ in range(2):
        nc = bacc.Bacc("TRN2", target_bir_lowering=False, num_devices=1)
        known = build_pass(nc, declare(nc, arrays), where, known)
    r = run_bass_kernel_spmd(nc, [{name + "_in": a for name, a in arrays.items()}], core_ids=[0]).results[0]
    return tuple(r[name + "_out"] for name in OUTPUTS)
```
